# Optimizing a Trainium2 kernel written in Bass

```python
import jax, jax.numpy as jnp
from jax import lax
import numpy as np

D_MODEL = 1024
BATCH = 1
SEQ = 1024
DEPTH = 1
DEC_BATCH = 1
DEC_SEQ = 64
PAST_LEN = 256

CHUNK = 64
N_META = 16
D_CONV = D_MODEL // 2
CONV_WIDTH = 3
RET_HEADS = 4
RET_HEAD_DIM = 128
D_RET = RET_HEADS * RET_HEAD_DIM
D_MIX = D_CONV + D_RET
D_FF = 4 * D_MODEL
ROPE_BASE = 10000.0
NORM_EPS = 1e-6
GN_EPS = 1e-5
D_IN = 3 * D_CONV + 4 * D_RET
IN_SPLITS = (D_CONV, 2 * D_CONV, 3 * D_CONV, 3 * D_CONV + D_RET, 3 * D_CONV + 2 * D_RET, 3 * D_CONV + 3 * D_RET)

kernel_name = "hymba_shortconv_retnet_stream_step"

def rmsnorm(x, w):
    xf = x.astype(jnp.float32)
    y = xf * lax.rsqrt(jnp.mean(xf * xf, axis=-1, keepdims=True) + NORM_EPS)
    return (y * w.astype(jnp.float32)).astype(x.dtype)

def rotary(x, pos):
    half = RET_HEAD_DIM // 2
    inv_freq = ROPE_BASE ** (-jnp.arange(half, dtype=jnp.float32) / half)
    ang = pos[:, None] * inv_freq[None, :]
    cos = jnp.cos(ang)[None, :, None, :]
    sin = jnp.sin(ang)[None, :, None, :]
    x1, x2 = x[..., :half], x[..., half:]
    return jnp.concatenate([x1 * cos - x2 * sin, x1 * sin + x2 * cos], axis=-1)

def retention_log_gamma():
    return jnp.log(1.0 - 2.0 ** (-5.0 - jnp.arange(RET_HEADS, dtype=jnp.float32)))

def retention_block(q, k, v, s, log_gamma):
    L = q.shape[1]
    idx = jnp.arange(L, dtype=jnp.float32)
    diff = idx[:, None] - idx[None, :]
    decay = jnp.where(diff[None] >= 0,
                      jnp.exp(jnp.maximum(diff, 0.0)[None] * log_gamma[:, None, None]), 0.0)
    scores = jnp.einsum("bihd,bjhd->bhij", q, k) * decay[None]
    inner = jnp.einsum("bhij,bjhe->bihe", scores, v)
    cross_decay = jnp.exp((idx + 1.0)[:, None] * log_gamma[None, :])
    cross = jnp.einsum("bihd,bhde->bihe", q, s) * cross_decay[None, :, :, None]
    k_decay = jnp.exp((L - 1.0 - idx)[:, None] * log_gamma[None, :])
    s_new = jnp.exp(L * log_gamma)[None, :, None, None] * s + jnp.einsum(
        "bjhd,bjhe,jh->bhde", k, v, k_decay)
    return inner + cross, s_new

def retention_seq(q, k, v, s, lead):
    log_gamma = retention_log_gamma()
    outs = []
    if lead > 0:
        o, s = retention_block(q[:, :lead], k[:, :lead], v[:, :lead], s, log_gamma)
        outs.append(o)
        q, k, v = q[:, lead:], k[:, lead:], v[:, lead:]
    bsz, T = q.shape[0], q.shape[1]
    if T <= CHUNK:
        o, s = retention_block(q, k, v, s, log_gamma)
        outs.append(o)
    else:
        nc = T // CHUNK

        def to_chunks(a):
            return a.reshape(bsz, nc, CHUNK, RET_HEADS, RET_HEAD_DIM).transpose(1, 0, 2, 3, 4)

        def step(state, qkv):
            qc, kc, vc = qkv
            oc, state = retention_block(qc, kc, vc, state, log_gamma)
            return state, oc

        s, o = lax.scan(step, s, (to_chunks(q), to_chunks(k), to_chunks(v)))
        outs.append(o.transpose(1, 0, 2, 3, 4).reshape(bsz, T, RET_HEADS, RET_HEAD_DIM))
    o = jnp.concatenate(outs, axis=1) if len(outs) > 1 else outs[0]
    return o, s

def hybrid_layer(h, pos, conv_hist, ret_state, lead,
                 norm_mix_w, w_in, conv_w, ret_gn_w, w_out, norm_ffn_w, w_up, w_down):
    bsz, T, _ = h.shape
    hn = rmsnorm(h, norm_mix_w)
    proj = hn @ w_in
    xt, b_gate, c_gate, q, k, v, g = jnp.split(proj, IN_SPLITS, axis=-1)
    ucat = jnp.concatenate([conv_hist.astype(h.dtype), c_gate * xt], axis=1)
    conv_y = conv_w[0] * ucat[:, :T] + conv_w[1] * ucat[:, 1:T + 1] + conv_w[2] * ucat[:, 2:]
    conv_out = b_gate * conv_y
    new_hist = ucat[:, T:]
    def heads(a):
        return a.astype(jnp.float32).reshape(bsz, T, RET_HEADS, RET_HEAD_DIM)
    qh = rotary(heads(q), pos)
    kh = rotary(heads(k), pos) * (RET_HEAD_DIM ** -0.5)
    vh = heads(v)
    o, new_state = retention_seq(qh, kh, vh, ret_state.astype(jnp.float32), lead)
    mu = jnp.mean(o, axis=-1, keepdims=True)
    var = jnp.mean(jnp.square(o - mu), axis=-1, keepdims=True)
    o = ((o - mu) * lax.rsqrt(var + GN_EPS)).reshape(bsz, T, D_RET) * ret_gn_w.astype(jnp.float32)
    ret_out = (jax.nn.silu(g.astype(jnp.float32)) * o).astype(h.dtype)
    h = h + jnp.concatenate([conv_out, ret_out], axis=-1) @ w_out
    f = jnp.square(jax.nn.relu(rmsnorm(h, norm_ffn_w) @ w_up)) @ w_down
    return h + f, new_hist, new_state.astype(h.dtype)

def setup_inputs(seed: int = 0) -> dict:
    key = jax.random.key(seed)
    ks = jax.random.split(key, 14)
    f32 = jnp.float32
    return {
        "x_prompt": jax.random.normal(ks[0], (BATCH, SEQ, D_MODEL), f32),
        "x_sample": jax.random.normal(ks[1], (DEC_BATCH, DEC_SEQ, D_MODEL), f32),
        "state_conv": jax.random.normal(ks[2], (DEPTH, DEC_BATCH, CONV_WIDTH - 1, D_CONV), f32),
        "state_ret": 0.5 * jax.random.normal(ks[3], (DEPTH, DEC_BATCH, RET_HEADS, RET_HEAD_DIM, RET_HEAD_DIM), f32),
        "meta_tokens": jax.random.normal(ks[4], (N_META, D_MODEL), f32),
        "norm_mix_w": 1.0 + 0.02 * jax.random.normal(ks[5], (DEPTH, D_MODEL), f32),
        "w_in": jax.random.normal(ks[6], (DEPTH, D_MODEL, D_IN), f32) * D_MODEL ** -0.5,
        "conv_w": jax.random.normal(ks[7], (DEPTH, CONV_WIDTH, D_CONV), f32) * CONV_WIDTH ** -0.5,
        "ret_gn_w": 1.0 + 0.02 * jax.random.normal(ks[8], (DEPTH, D_RET), f32),
        "w_out": jax.random.normal(ks[9], (DEPTH, D_MIX, D_MODEL), f32) * D_MIX ** -0.5,
        "norm_ffn_w": 1.0 + 0.02 * jax.random.normal(ks[10], (DEPTH, D_MODEL), f32),
        "w_up": jax.random.normal(ks[11], (DEPTH, D_MODEL, D_FF), f32) * D_MODEL ** -0.5,
        "w_down": jax.random.normal(ks[12], (DEPTH, D_FF, D_MODEL), f32) * D_FF ** -0.5,
        "norm_final_w": 1.0 + 0.02 * jax.random.normal(ks[13], (D_MODEL,), f32),
    }

def reference(x_prompt, x_sample, state_conv, state_ret, meta_tokens, norm_mix_w, w_in, conv_w,
              ret_gn_w, w_out, norm_ffn_w, w_up, w_down, norm_final_w):
    bp = x_prompt.shape[0]
    meta = jnp.broadcast_to(meta_tokens[None].astype(x_prompt.dtype), (bp, N_META, D_MODEL))
    hp = jnp.concatenate([meta, x_prompt], axis=1)
    pos_p = jnp.arange(hp.shape[1], dtype=jnp.float32) - float(N_META)
    hs = x_sample
    pos_s = jnp.arange(x_sample.shape[1], dtype=jnp.float32) + float(PAST_LEN)
    zero_hist = jnp.zeros((bp, CONV_WIDTH - 1, D_CONV), x_prompt.dtype)
    zero_ret = jnp.zeros((bp, RET_HEADS, RET_HEAD_DIM, RET_HEAD_DIM), jnp.float32)
    conv_p, ret_p, conv_s, ret_s = [], [], [], []
    for l in range(DEPTH):
        params = (norm_mix_w[l], w_in[l], conv_w[l], ret_gn_w[l], w_out[l], norm_ffn_w[l], w_up[l], w_down[l])
        hp, cp, rp = hybrid_layer(hp, pos_p, zero_hist, zero_ret, N_META, *params)
        hs, cs, rs = hybrid_layer(hs, pos_s, state_conv[l], state_ret[l], 0, *params)
        conv_p.append(cp)
        ret_p.append(rp)
        conv_s.append(cs)
        ret_s.append(rs)
    y_prompt = rmsnorm(hp[:, N_META:], norm_final_w)
    y_sample = rmsnorm(hs, norm_final_w)
    return (y_prompt, y_sample, jnp.stack(conv_p), jnp.stack(ret_p), jnp.stack(conv_s), jnp.stack(ret_s))


_drawn_inputs = setup_inputs


def setup_inputs(seed=0):
    import zlib

    import numpy as np

    out = dict(_drawn_inputs(seed))
    spreads = {}
    factors = {'ret_gn_w': 21.857, 'norm_ffn_w': 10.561, 'norm_final_w': 20.413, 'state_conv': 5.04}
    for name, (base, spread) in spreads.items():
        noise = np.random.default_rng([zlib.crc32(name.encode()), seed]).standard_normal(out[name].shape)
        drawn = base * np.exp(spread * noise) if base else spread * noise
        out[name] = __import__('jax').numpy.asarray(drawn.astype(out[name].dtype))
    for name, factor in factors.items():
        out[name] = (out[name] * factor).astype(out[name].dtype)
    return out
```

```python
from contextlib import ExitStack

import numpy as np

import concourse.bass as bass
from concourse import mybir

F32 = mybir.dt.float32
F32R = mybir.dt.float32r
ALU = mybir.AluOpType
ACT = mybir.ActivationFunctionType

P = 128
D = 1024
SEQ = 1024
SAMPLE = 64
PAST = 256
META = 16
DC = 512
HEADS = 4
HD = 128
FF = 4 * D
DIN = 3 * DC + 4 * HEADS * HD
EPS = 1e-6
GN_EPS = 1e-5

KT = D // P
TX = META + SEQ + SAMPLE
TY = SEQ + SAMPLE
TILES = (TY + P - 1) // P
XTILES = (TX + P - 1) // P
BLK = 368
CGX = [(0, 368), (368, 368), (736, 368)]
CGQ = [(16, 352), (368, 368), (736, 368)]
CGY = [(0, 368), (368, 368), (736, 352)]

UNITS = [("v", 3 * DC + 2 * DC, CGX), ("k", 3 * DC + DC, CGX), ("q", 3 * DC, CGQ),
         ("g", 3 * DC + 3 * DC, CGQ), ("xt", 0, CGX), ("c", 2 * DC, CGX), ("b", DC, CGQ)]
NU = len(UNITS)
HALVES = 2 * NU
STEPS = ["vA", "vB", "vC", "kC", "UC", "kA", "UA", "sC", "sA", "oC", "oA", "kB", "UB", "tC", "tA",
         "sB", "oB", "tB"]
AFTER = {(1, 1): "vA", (1, 2): "vB", (1, 3): "vC", (2, 2): "kC", (2, 3): "UC", (2, 4): "kA",
         (2, 5): "UA", (3, 2): "sC", (3, 3): "sA", (3, 4): "oC", (3, 5): "oA", (4, 0): "kB",
         (4, 1): "UB", (4, 2): "tC", (4, 3): "tA", (4, 4): "sB", (5, 1): "oB", (5, 5): "tB"}
NS = len(STEPS)
BY_ACT = ["vA", "vB", "vC", "kC", "kA", "kB"]
BY_DVE = [s for s in STEPS if s not in BY_ACT]
ACT_UNITS = ["v", "g", "xt"]
DVE_UNITS = ["k", "q", "c", "b"]
MIX_PARTS = ["tC", "tA", "tB", 0, 1, 2]
KORDER = [4, 5, 6, 7, 0, 1, 2, 3]
GROUPS = 8
FT = FF // GROUPS // P
C_MASK, C_KDEC, C_KMETA, C_KSAMP, C_C, C_C2, C_G128, C_G64, NCONST = 0, 128, 129, 130, 131, 132, 133, 134, 135


def constants():
    half = HD // 2
    inv = (np.float32(10000.0) ** (-np.arange(half, dtype=np.float32) / np.float32(half))).astype(np.float32)
    pos = np.concatenate([np.arange(META + SEQ) - META, np.arange(SAMPLE) + PAST]).astype(np.float32)
    ang = (pos[None, :] * inv[:, None]).astype(np.float32).astype(np.float64)
    cos = np.concatenate([np.cos(ang), np.cos(ang)]).astype(np.float32)
    sin = np.concatenate([-np.sin(ang), np.sin(ang)]).astype(np.float32)
    head = np.zeros((HEADS, P, NCONST), np.float64)
    j = np.arange(P)
    scale = HD ** -0.5
    for h in range(HEADS):
        lg = np.log(1.0 - 2.0 ** (-5.0 - h))
        head[h, :, :P] = np.where(j[None, :] >= j[:, None], np.exp(-(j[:, None] + 1) * lg), 0.0) * scale
        head[h, :, C_KDEC] = np.exp((P - 1 - j) * lg) * scale
        head[h, :META, C_KMETA] = np.exp((META - 1 - j[:META]) * lg) * scale
        head[h, :SAMPLE, C_KSAMP] = np.exp((SAMPLE - 1 - j[:SAMPLE]) * lg) * scale
        head[h, :, C_C] = np.exp((j + 1) * lg)
        head[h, :, C_C2] = np.exp(2 * (j + 1) * lg)
        head[h, :, C_G128] = np.exp(P * lg)
        head[h, :, C_G64] = np.exp(SAMPLE * lg)
    return {"c_cos": cos, "c_sin": sin, "c_head": head.astype(np.float32), "c_ident": np.eye(P, dtype=np.float32)}


def build(nc, x_prompt, x_sample, state_conv, state_ret, meta_tokens, norm_mix_w, w_in, conv_w, ret_gn_w,
          w_out, norm_ffn_w, w_up, w_down, norm_final_w, c_cos, c_sin, c_head, c_ident,
          y_prompt, y_sample, new_conv_prompt, new_ret_prompt, new_conv_sample, new_ret_sample):
    ctx = ExitStack()
    with ctx:
        base = (nc.sbuf_base + 31) // 32 * 32
        place = {"at": base}

        def region(size):
            at = place["at"]
            place["at"] = at + (size + 31) // 32 * 32
            return at

        def sb(name, shape, at, dt=F32):
            return nc.alloc_sbuf_tensor_at(name, shape, dt, offset=at)

        r1 = region(2 * KT * TX * 4)
        hn_hi = sb("hn_hi", [P, KT, TX], r1, F32R)
        hn_lo = sb("hn_lo", [P, KT, TX], r1 + KT * TX * 4, F32R)
        wo_hi = sb("wo_hi", [P, KT, D], r1, F32R)
        wo_lo = sb("wo_lo", [P, KT, D], r1 + KT * D * 4, F32R)
        f_hi = sb("f_hi", [P, FT, TY], r1, F32R)
        f_lo = sb("f_lo", [P, FT, TY], r1 + FT * TY * 4, F32R)
        wd_hi = sb("wd_hi", [P, FT, D], r1 + 2 * FT * TY * 4, F32R)
        wd_lo = sb("wd_lo", [P, FT, D], r1 + 2 * FT * TY * 4 + FT * D * 4, F32R)
        r2 = region(2 * KT * TY * 4)
        xr = sb("xr", [P, 4, D], r2)
        mid_hi = sb("mid_hi", [P, KT, TY], r2, F32R)
        mid_lo = sb("mid_lo", [P, KT, TY], r2 + KT * TY * 4, F32R)
        ws_hi = sb("ws_hi", [P, 2, 4, P], region(4096), F32R)
        ws_lo = sb("ws_lo", [P, 2, 4, P], region(4096), F32R)
        raw = sb("raw", [P, 4, 512], region(8192))
        normw = sb("normw", [P, D], region(4096))
        ident = sb("ident", [P, P], region(512))
        bn = sb("bn", [P, 4, 6], region(96))
        mv = sb("mv", [P, 2], region(8))
        gs = sb("gs", [P, 3, 4], region(48))
        small = sb("small", [P, 4, 4], region(64))
        inv_ms = sb("inv_ms", [P, TILES], region(36))
        r3 = place["at"]

        cos_t = sb("cos_t", [P, TX], region(TX * 4))
        sin_t = sb("sin_t", [P, TX], region(TX * 4))
        qT = sb("qT", [P, TY], region(TY * 4))
        kT = sb("kT", [P, TX], region(TX * 4))
        vg = sb("vg", [P, TX], region(TX * 4))
        v_tok = sb("v_tok", [P, 10, HD], region(10 * HD * 4))
        u = sb("u", [P, TX + 2], region((TX + 2) * 4))
        y = sb("y", [P, TY], region(TY * 4))
        sm = sb("sm", [P, 4, P], region(2048))
        kd = sb("kd", [P, 4, HD], region(2048))
        on = sb("on", [P, 4, HD], region(2048))
        st = sb("st", [P, 5, HD], region(2560))
        smC = sb("smC", [P, SAMPLE], region(256))
        onC = sb("onC", [P, HD], region(512))
        kdC = sb("kdC", [P, 2, HD], region(1024))
        s_in = sb("s_in", [P, HD], region(512))
        s_new = sb("s_new", [P, HD], region(512))
        rot = sb("rot", [P, BLK], region(BLK * 4))
        hc = sb("hc", [P, NCONST], region(NCONST * 4))
        gnw = sb("gnw", [P, 1], region(4))
        cw = sb("cw", [P, 3], region(12))
        hist = sb("hist", [P, 2], region(8))
        ncp = sb("ncp", [P, HEADS, 2], region(32))
        ncs = sb("ncs", [P, HEADS, 2], region(32))
        end2 = place["at"]

        place["at"] = r3
        h = sb("h", [P, TILES, D], region(TILES * D * 4))
        hw = sb("hw", [P, 2, D], region(2 * D * 4))
        rl = sb("rl", [P, 2, BLK], region(2 * BLK * 4))
        sq = sb("sq", [P, 2, BLK], region(2 * BLK * 4))
        assert max(end2, place["at"]) <= nc.sbuf_usable_end, (end2, place["at"], nc.sbuf_usable_end)

        ps = [ctx.enter_context(nc.psum_tensor(f"ps{n}", [P, 512], F32)) for n in range(8)]
        T_PAIRS = [(4, 5), (6, 7)]
        RET = [6, 7]
        PAIRS3 = [(4, 5), (6, 7), (0, 1), (2, 3)]
        DOWN_PAIRS = [(0, 1), (2, 3), (6, 7)]

        def sem(name):
            return ctx.enter_context(nc.semaphore(name))

        const_in = sem("const_in")
        rope_in = sem("rope_in")
        x_in = [sem(f"x_in{n}") for n in range(4)]
        ms_ready = sem("ms_ready")
        sd_ready = sem("sd_ready")
        xn_ready = sem("xn_ready")
        xt_done = sem("xt_done")
        hn_hi_ready = sem("hn_hi_ready")
        hn_ready = sem("hn_ready")
        raw_in = [sem(f"raw_in{n}") for n in range(4)]
        w_hi = sem("w_hi")
        w_split = sem("w_split")
        w_used = sem("w_used")
        proj_done = sem("proj_done")
        proj_act = sem("proj_act")
        proj_dve = sem("proj_dve")
        ret_done = sem("ret_done")
        ret_act = sem("ret_act")
        ret_dve = sem("ret_dve")
        head_in = sem("head_in")
        var_ready = sem("var_ready")
        gsd_ready = sem("gsd_ready")
        mix_hi_ready = sem("mix_hi_ready")
        mix_ready = sem("mix_ready")
        s_new_out = sem("s_new_out")
        s_end_out = sem("s_end_out")
        conv_out = sem("conv_out")
        normw_in = sem("normw_in")
        h_in = sem("h_in")
        h_rest_in = sem("h_rest_in")
        out_done = sem("out_done")
        out_taken = sem("out_taken")
        hw_ready = sem("hw_ready")
        ht_done = sem("ht_done")
        ht_hi_ready = sem("ht_hi_ready")
        ht_ready = sem("ht_ready")
        ms2_ready = sem("ms2_ready")
        up_done = sem("up_done")
        relu_done = sem("relu_done")
        sq_done = sem("sq_done")
        f_hi_ready = sem("f_hi_ready")
        f_ready = sem("f_ready")
        down_done = sem("down_done")
        down_taken = sem("down_taken")
        fin_ms = sem("fin_ms")
        fin_sd = sem("fin_sd")
        y_ready = sem("y_ready")
        y_out = [sem("y_out0"), sem("y_out1")]
        dve_step = sem("dve_step")
        NX = 3

        w_in_t = w_in[0].rearrange("(k p) n -> p k n", p=P)
        w_up_t = w_up[0].rearrange("(k p) n -> p k n", p=P)
        w_out_t = w_out[0].rearrange("(k p) n -> p k n", p=P)
        w_down_t = w_down[0].rearrange("(k p) n -> p k n", p=P)
        meta_d, xp_d, xs_d = meta_tokens, x_prompt[0], x_sample[0]

        def x_rows(t):
            lo, hi = t * P, min((t + 1) * P, TX)
            out = []
            for src, a, b in ((meta_d, 0, META), (xp_d, META, META + SEQ), (xs_d, META + SEQ, TX)):
                s, e = max(lo, a), min(hi, b)
                if s < e:
                    out.append((src[s - a:e - a, :], s - lo, e - s))
            return out

        def rows(t):
            return min(P, TY - t * P)

        def xrows(t):
            return min(P, TX - t * P)

        X_COUNT = []
        seen = [0] * 4
        for t in range(XTILES):
            seen[t % 4] += 16 * len(x_rows(t))
            X_COUNT.append(seen[t % 4])

        def n_step(name):
            return STEPS.index(name) + 1

        def n_act(name):
            return BY_ACT.index(name) + 1

        def n_dve(name):
            return BY_DVE.index(name) + 1

        H_OUT = HALVES * HEADS
        H_FFN = H_OUT + 2 * KT
        FFN_ORDER = []
        for p in range(1, 7):
            FFN_ORDER += [("wd", (p - 1) // 2, (p - 1) % 2), ("up", (p + 1) // 2, (p + 1) % 2)]
        FFN_ORDER += [("wd", 3, 0), ("wd", 3, 1), ("next", 0, 0), ("next", 0, 1)]
        NF = len(FFN_ORDER)
        assert NF == 4 * FT

        def ffn_half(kind, a, half):
            return H_FFN + 2 + FFN_ORDER.index((kind, a, half)) if (kind, a) != ("up", 0) else H_FFN + half

        def raw_slot(n):
            if n < H_OUT:
                return n % 2, n // 2
            m = n - H_OUT
            s = (m + 2) % 4
            return s, m // 4 + (H_OUT // 2 if s < 2 else 0)

        block = ctx.enter_context(nc.Block())

        @block.sync
        def _(sp):
            sp.dma_start(ident[:, :], c_ident).then_inc(const_in, 16)
            sp.dma_start(normw[:, :], norm_mix_w[0:1, :].broadcast_to([P, D])).then_inc(const_in, 16)

            def load_x(t):
                if t >= 4:
                    sp.wait_ge(xt_done, t - 3)
                for src, at, n in x_rows(t):
                    sp.dma_start(xr[at:at + n, t % 4, :], src).then_inc(x_in[t % 4], 16)

            def load_in(i, n):
                off = UNITS[n // 2][1] + i * P
                sp.dma_start(raw[:, n % 2, :].rearrange("p (k c) -> p k c", k=4),
                             w_in_t[:, 4 * (n % 2):4 * (n % 2) + 4, bass.ds(off, P)]).then_inc(raw_in[n % 2], 16)

            def iteration(i, first):
                for n in range(HALVES):
                    if not (first and n < 2):
                        sp.wait_ge(w_split, i * HALVES + n - 1)
                        load_in(i, n)
                    if n == 3:
                        sp.wait_ge(proj_dve, NX + i * 12)
                        sp.dma_start(hc[:, :], c_head[bass.ds(i, 1), :, :].rearrange("a p c -> p (a c)")).then_inc(head_in, 16)
                        sp.dma_start(s_in[:, :], state_ret[0, 0, bass.ds(i, 1), :, :].rearrange("a p c -> p (a c)")).then_inc(head_in, 16)
                        sp.dma_start(gnw[:, :], ret_gn_w[0:1, bass.ds(i * P, P)].rearrange("a p -> p a")).then_inc(head_in, 16)
                        sp.dma_start(cw[:, :], conv_w[0, :, bass.ds(i * P, P)].rearrange("w p -> p w"), allow_slow_non_contiguous=True).then_inc(head_in, 16)
                        sp.dma_start(hist[:, :], state_conv[0, 0, :, bass.ds(i * P, P)].rearrange("w p -> p w"), allow_slow_non_contiguous=True).then_inc(head_in, 16)
                    if n == 9:
                        sp.wait_ge(ret_dve, i * len(BY_DVE) + n_dve("UC"))
                        sp.dma_start(new_ret_sample[0, 0, bass.ds(i, 1), :, :].rearrange("a p c -> p (a c)"), s_new[:, :]).then_inc(s_new_out, 16)
                    if n == 12:
                        sp.wait_ge(ret_dve, i * len(BY_DVE) + n_dve("UB"))
                        sp.dma_start(new_ret_prompt[0, 0, bass.ds(i, 1), :, :].rearrange("a p c -> p (a c)"), st[:, 8 % 5, :]).then_inc(s_end_out, 16)

            for t in range(3):
                load_x(t)
            load_in(0, 0)
            load_in(0, 1)
            for t in range(3, XTILES):
                load_x(t)
            sp.dma_start(cos_t[:, :], c_cos).then_inc(rope_in, 16)
            sp.dma_start(sin_t[:, :], c_sin).then_inc(rope_in, 16)
            sp.wait_ge(xn_ready, XTILES)
            sp.dma_start(normw[:, :], norm_ffn_w[0:1, :].broadcast_to([P, D])).then_inc(normw_in, 16)
            iteration(0, True)
            with sp.Fori(1, HEADS) as i:
                iteration(i, False)

            def load_out(m):
                s, _ = raw_slot(H_OUT + m)
                if m >= 2:
                    sp.wait_ge(w_split, H_OUT + m - 3)
                k, nh = KORDER[m // 2], m % 2
                sp.dma_start(raw[:, s, :], w_out_t[:, k, nh * 512:nh * 512 + 512]).then_inc(raw_in[s], 16)

            for m in range(2 * KT):
                load_out(m)
                if m == 3:
                    sp.wait_ge(mix_ready, len(MIX_PARTS) * HEADS)
                    sp.wait_ge(s_new_out, 1 + 16 * HEADS)
                    sp.wait_ge(s_end_out, 1 + 16 * HEADS)
                    sp.dma_start(new_conv_prompt[0, 0].rearrange("w (i p) -> p i w", p=P)[:, :, 0], ncp[:, :, 0], allow_slow_non_contiguous=True).then_inc(conv_out, 16)
                    sp.dma_start(new_conv_prompt[0, 0].rearrange("w (i p) -> p i w", p=P)[:, :, 1], ncp[:, :, 1], allow_slow_non_contiguous=True).then_inc(conv_out, 16)
                    sp.dma_start(new_conv_sample[0, 0].rearrange("w (i p) -> p i w", p=P)[:, :, 0], ncs[:, :, 0], allow_slow_non_contiguous=True).then_inc(conv_out, 16)
                    sp.dma_start(new_conv_sample[0, 0].rearrange("w (i p) -> p i w", p=P)[:, :, 1], ncs[:, :, 1], allow_slow_non_contiguous=True).then_inc(conv_out, 16)
                    sp.dma_start(h[:, 0:2, :], xp_d[0:2 * P, :].rearrange("(t p) n -> p t n", p=P)).then_inc(h_in, 16)
            sp.wait_ge(conv_out, 64)
            sp.dma_start(h[:, 2:8, :], xp_d[2 * P:, :].rearrange("(t p) n -> p t n", p=P)).then_inc(h_rest_in, 16)
            sp.dma_start(h[0:SAMPLE, 8, :], xs_d).then_inc(h_rest_in, 16)

            def load_ffn(g, kind, a, half, n, extra):
                s, _ = raw_slot(n)
                sp.wait_ge(w_split, n - 3 + extra)
                if kind == "wd":
                    src = w_down_t[:, bass.ds(g * FT + a, 1), half * 512:half * 512 + 512].rearrange("p a c -> p (a c)")
                    sp.dma_start(raw[:, s, :], src).then_inc(raw_in[s], 16)
                else:
                    col = (g * FT + a + (FT if kind == "next" else 0)) * P
                    sp.dma_start(raw[:, s, :].rearrange("p (k c) -> p k c", k=4),
                                 w_up_t[:, 4 * half:4 * half + 4, bass.ds(col, P)]).then_inc(raw_in[s], 16)

            def group(g, last):
                for kind, a, half in FFN_ORDER:
                    if not (last and kind == "next"):
                        load_ffn(g, kind, a, half, ffn_half(kind, a, half), g * NF)

            for half in range(2):
                load_ffn(0, "up", 0, half, H_FFN + half, 0)
            with sp.Fori(0, GROUPS - 1) as g:
                group(g, False)
            sp.wait_ge(hw_ready, TILES)
            sp.dma_start(normw[:, :], norm_final_w.rearrange("(a n) -> a n", a=1).broadcast_to([P, D])).then_inc(normw_in, 16)
            group(GROUPS - 1, True)
            for t in range(TILES):
                sp.wait_ge(y_ready, t + 1)
                dst = y_prompt[0, t * P:(t + 1) * P, :] if t < SEQ // P else y_sample[0]
                sp.dma_start(dst, hw[0:rows(t), t % 2, :]).then_inc(y_out[t % 2], 16)
            sp.wait_ge(y_out[0], 16 * ((TILES + 1) // 2))
            sp.wait_ge(y_out[1], 16 * (TILES // 2))

        @block.scalar
        def _(act):
            def split_in(i, n):
                s = n % 2
                act.wait_ge(raw_in[s], 16 * (i * (HALVES // 2) + n // 2 + 1))
                if n >= 2 and s == 0:
                    act.wait_ge(w_used, i * NU + n // 2)
                elif n >= 2:
                    act.wait_ge(proj_done, i * 3 * NU + 3 * (n // 2))
                act.activation(ws_hi[:, s], raw[:, s, :].rearrange("p (k c) -> p k c", k=4), ACT.Copy).then_inc(w_hi, 1)

            def root(t):
                act.wait_ge(ms_ready, t + 1)
                n = xrows(t)
                act.activation(small[0:n, t % 4, 1:2], small[0:n, t % 4, 0:1], ACT.Sqrt).then_inc(sd_ready, 1)

            def hi_parts(t):
                n = xrows(t)
                act.wait_ge(xt_done, t + 1)
                for b in range(2):
                    last = act.activation(hn_hi[:, 4 * b:4 * b + 4, t * P:t * P + n],
                                          ps[T_PAIRS[t % 2][b]][:, 0:4 * n].rearrange("p (k c) -> p k c", k=4), ACT.Copy)
                last.then_inc(hn_hi_ready, 1)

            root(0)
            for t in range(XTILES):
                if t + 1 < XTILES:
                    root(t + 1)
                hi_parts(t)
                if t == 2:
                    split_in(0, 0)
                    split_in(0, 1)

            def take_unit(i, uname, j):
                act.wait_ge(proj_done, i * 3 * NU + 3 * [x[0] for x in UNITS].index(uname) + j + 1)
                set0 = [x[0] for x in UNITS].index(uname) % 2 * 3
                col, n = dict((x[0], x[2]) for x in UNITS)[uname][j]
                bank = ps[set0 + j]
                if uname == "v":
                    if j == 0:
                        act.wait_ge(proj_dve, NX + i * 12)
                    act.activation(vg[:, col:col + n], bank[:, 0:n], ACT.Copy).then_inc(proj_act, 1)
                elif uname == "g":
                    if j == 0:
                        act.wait_ge(ret_done, i * NS + n_step("vC"))
                    act.activation(vg[:, col:col + n], bank[:, 0:n], ACT.Silu).then_inc(proj_act, 1)
                else:
                    if j == 0:
                        act.wait_ge(proj_dve, NX + i * 12)
                    if j < 2:
                        act.activation(u[:, col:col + n], bank[:, 0:n], ACT.Copy).then_inc(proj_act, 1)
                    else:
                        m = META + SEQ - col
                        act.activation(u[:, col:col + m], bank[:, 0:m], ACT.Copy)
                        act.activation(u[:, col + m + 2:TX + 2], bank[:, m:n], ACT.Copy).then_inc(proj_act, 1)

            def take_step(i, name):
                bank = ps[RET[STEPS.index(name) % 2]]
                if name in BY_ACT:
                    act.wait_ge(ret_done, i * NS + n_step(name))
                if name in ("vA", "vB"):
                    c = 0 if name == "vA" else 4
                    act.activation(v_tok[:, c:c + 4, :], bank[:, :].rearrange("p (c e) -> p c e", c=4), ACT.Copy).then_inc(ret_act, 1)
                elif name == "vC":
                    act.activation(v_tok[0:META, 8, :], bank[0:META, 0:HD], ACT.Copy)
                    act.activation(v_tok[0:SAMPLE, 9, :], bank[0:SAMPLE, HD:2 * HD], ACT.Copy).then_inc(ret_act, 1)
                elif name == "kC":
                    act.wait_ge(head_in, 16 * 5 * (i + 1))
                    act.activation(kdC[0:META, 0, :], bank[0:META, 0:HD], ACT.Copy, scale=hc[0:META, C_KMETA:C_KMETA + 1])
                    act.activation(kdC[0:SAMPLE, 1, :], bank[0:SAMPLE, HD:2 * HD], ACT.Copy,
                                   scale=hc[0:SAMPLE, C_KSAMP:C_KSAMP + 1]).then_inc(ret_act, 1)
                elif name in ("kA", "kB"):
                    act.activation(kd[:, :, :], bank[:, :].rearrange("p (c e) -> p c e", c=4), ACT.Copy,
                                   scale=hc[:, C_KDEC:C_KDEC + 1]).then_inc(ret_act, 1)
                elif name in ("oC", "oA", "oB"):
                    w, n = (1, SAMPLE) if name == "oC" else (4, P)
                    act.wait_ge(var_ready, i * 3 + ["oC", "oA", "oB"].index(name) + 1)
                    act.activation(small[0:n, 1, 0:w], small[0:n, 0, 0:w], ACT.Sqrt).then_inc(gsd_ready, 1)
                elif name in ("tC", "tA", "tB"):
                    act.wait_ge(ret_dve, i * len(BY_DVE) + n_dve(name))
                    col, n = {"tC": (SEQ, SAMPLE), "tA": (0, 512), "tB": (512, 512)}[name]
                    src = onC[:, 0:SAMPLE] if name == "tC" else on[:, :, :].rearrange("p c e -> p (c e)")
                    act.activation(mid_hi[:, bass.ds(i + 4, 1), col:col + n].rearrange("p a c -> p (a c)"), src, ACT.Copy).then_inc(mix_hi_ready, 1)

            def conv_hi(i, j):
                act.wait_ge(proj_dve, NX + i * 12 + 9 + j + 1)
                col, n = CGQ[j]
                act.activation(mid_hi[:, bass.ds(i, 1), col - META:col - META + n].rearrange("p a c -> p (a c)"),
                               y[:, col - META:col - META + n], ACT.Copy).then_inc(mix_hi_ready, 1)

            def iteration(i, last):
                for un in range(NU):
                    for b in range(6):
                        half = 2 * un + b // 3
                        if b % 3 == 0 and half >= 1 and not (last and half + 1 == HALVES):
                            split_in(i, half + 1)
                        if b >= 3 and UNITS[un][0] in ACT_UNITS:
                            take_unit(i, UNITS[un][0], b - 3)
                        if b >= 3 and UNITS[un][0] == "b":
                            conv_hi(i, b - 3)
                        if (un, b) in AFTER:
                            take_step(i, AFTER[un, b])
                if not last:
                    split_in(i, HALVES + 1)

            with act.Fori(0, HEADS - 1) as i:
                iteration(i, False)
            iteration(HEADS - 1, True)

            act.wait_ge(proj_done, 3 * NU * HEADS)
            for m in range(2 * KT):
                s, before = raw_slot(H_OUT + m)
                act.wait_ge(raw_in[s], 16 * (before + 1))
                act.activation(wo_hi[:, KORDER[m // 2], m % 2 * 512:m % 2 * 512 + 512], raw[:, s, :], ACT.Copy).then_inc(w_hi, 1)

            def ht_hi(t):
                n = rows(t)
                act.wait_ge(ht_done, t + 1)
                for b in range(2):
                    last = act.activation(mid_hi[:, 4 * b:4 * b + 4, t * P:t * P + n],
                                          ps[PAIRS3[(2 * t + 2) % 4][b]][:, 0:4 * n].rearrange("p (k c) -> p k c", k=4), ACT.Copy)
                last.then_inc(ht_hi_ready, 1)

            def split_ffn(g, kind, a, half):
                n = ffn_half(kind, a, half)
                s, before = raw_slot(n)
                act.wait_ge(raw_in[s], 16 * (before + 1) + g * (16 * NF // 4))
                if kind == "wd":
                    act.activation(wd_hi[:, a, half * 512:half * 512 + 512], raw[:, s, :], ACT.Copy).then_inc(w_hi, 1)
                else:
                    act.activation(ws_hi[:, half], raw[:, s, :].rearrange("p (k c) -> p k c", k=4), ACT.Copy).then_inc(w_hi, 1)

            for t in range(TILES):
                ht_hi(t)
                if t == 2:
                    split_ffn(0, "up", 0, 0)
                    split_ffn(0, "up", 0, 1)

            def group(g, last):
                for p in range(8):
                    if 1 <= p:
                        if p % 2 == 1:
                            act.wait_ge(w_used, NU * HEADS + FT * g + p // 2 + 1)
                        else:
                            act.wait_ge(up_done, 12 * g + 3 * (p // 2))
                        split_ffn(g, *FFN_ORDER[2 * p - 2])
                        split_ffn(g, *FFN_ORDER[2 * p - 1])
                    if p % 2 == 1:
                        a = p // 2
                        for j in range(3):
                            n = 3 * a + j
                            w = CGY[j][1]
                            act.wait_ge(up_done, 12 * g + n + 1)
                            act.activation(rl[:, n % 2, 0:w], ps[a % 2 * 3 + j][:, 0:w], ACT.Relu).then_inc(relu_done, 1)
                            act.wait_ge(sq_done, 12 * g + n + 1)
                            act.activation(f_hi[:, a, CGY[j][0]:CGY[j][0] + w], sq[:, n % 2, 0:w], ACT.Copy).then_inc(f_hi_ready, 1)
                if not last:
                    act.wait_ge(up_done, 12 * g + 12)
                    split_ffn(g, "next", 0, 0)
                    split_ffn(g, "next", 0, 1)
                else:
                    for t in range(TILES):
                        act.wait_ge(fin_ms, t + 1)
                        n = rows(t)
                        act.activation(small[0:n, t % 4, 1:2], small[0:n, t % 4, 0:1], ACT.Sqrt).then_inc(fin_sd, 1)

            with act.Fori(0, GROUPS - 1) as g:
                group(g, False)
            group(GROUPS - 1, True)

        @block.vector
        def _(dve):
            chain = {"n": 0, "base": 0}

            def link(ins):
                chain["n"] += 1
                ins.then_inc(dve_step, 1)
                dve.wait_ge(dve_step, chain["n"] + chain["base"])

            def mean_square(src, n, slot, eps=EPS):
                dve.bn_stats(bn[0:n, 0, :], src[:, 0:512])
                link(dve.bn_stats(bn[0:n, 1, :], src[:, 512:1024]))
                link(dve.bn_aggr(mv[0:n, :], bn[0:n, 0:2, :]))
                link(dve.scalar_tensor_tensor(small[0:n, slot, 0:1], mv[0:n, 0:1], mv[0:n, 0:1], mv[0:n, 1:2], ALU.mult, ALU.add))
                return dve.tensor_scalar(small[0:n, slot, 0:1], small[0:n, slot, 0:1], eps, None, ALU.add)

            def split_in(i, n):
                dve.wait_ge(w_hi, i * HALVES + n + 1)
                s = n % 2
                dve.tensor_tensor(ws_lo[:, s], raw[:, s, :].rearrange("p (k c) -> p k c", k=4),
                                  ws_hi[:, s].bitcast(F32), ALU.subtract).then_inc(w_split, 1)

            dve.sem_inc(proj_dve, NX)
            dve.sem_inc(down_taken, 2)
            dve.sem_inc(s_new_out, 1)
            dve.sem_inc(s_end_out, 1)
            dve.wait_ge(const_in, 32)

            def stats(t):
                n = xrows(t)
                dve.wait_ge(x_in[t % 4], X_COUNT[t])
                mean_square(xr[0:n, t % 4, :], n, t % 4).then_inc(ms_ready, 1)

            def normed(t):
                n = xrows(t)
                dve.wait_ge(sd_ready, t + 1)
                link(dve.reciprocal(small[0:n, t % 4, 2:3], small[0:n, t % 4, 1:2]))
                dve.scalar_tensor_tensor(xr[0:n, t % 4, :], xr[0:n, t % 4, :], small[0:n, t % 4, 2:3], normw[0:n, :],
                                         ALU.mult, ALU.mult).then_inc(xn_ready, 1)

            def lo_parts(t):
                n = xrows(t)
                dve.wait_ge(hn_hi_ready, t + 1)
                for b in range(2):
                    sl = (slice(None), slice(4 * b, 4 * b + 4), slice(t * P, t * P + n))
                    last = dve.tensor_tensor(hn_lo[sl], ps[T_PAIRS[t % 2][b]][:, 0:4 * n].rearrange("p (k c) -> p k c", k=4),
                                             hn_hi[sl].bitcast(F32), ALU.subtract)
                last.then_inc(hn_ready, 1)

            stats(0)
            normed(0)
            for t in range(XTILES):
                if t + 1 < XTILES:
                    stats(t + 1)
                    normed(t + 1)
                lo_parts(t)
                if t == 2:
                    split_in(0, 0)
                    split_in(0, 1)
            dve.wait_ge(rope_in, 32)
            link(dve.memset(onC[:, :], 0.0))

            names = [x[0] for x in UNITS]

            def rotary(dst, bank, col, n, at, before):
                dve.tensor_tensor(dst[:, at:at + n], bank[:, 0:n], cos_t[:, col:col + n], ALU.mult)
                dve.wait_ge(proj_dve, before)
                dve.tensor_tensor(rot[0:64, 0:n], bank[64:128, 0:n], sin_t[0:64, col:col + n], ALU.mult)
                link(dve.tensor_tensor(rot[64:128, 0:n], bank[0:64, 0:n], sin_t[64:128, col:col + n], ALU.mult))
                return dve.tensor_tensor(dst[:, at:at + n], dst[:, at:at + n], rot[:, 0:n], ALU.add)

            def take_unit(i, uname, j):
                un = names.index(uname)
                dve.wait_ge(proj_done, i * 3 * NU + 3 * un + j + 1)
                bank = ps[un % 2 * 3 + j]
                col, n = UNITS[un][2][j]
                if uname == "k":
                    rotary(kT, bank, col, n, col, NX + i * 12 + j).then_inc(proj_dve, 1)
                elif uname == "q":
                    rotary(qT, bank, col, n, col - META, NX + i * 12 + 3 + j).then_inc(proj_dve, 1)
                elif uname == "c":
                    dve.wait_ge(proj_act, i * 9 + 6 + j + 1)
                    m = min(n, META + SEQ - col)
                    ins = dve.tensor_tensor(u[:, col:col + m], bank[:, 0:m], u[:, col:col + m], ALU.mult)
                    if m < n:
                        ins = dve.tensor_tensor(u[:, col + m + 2:TX + 2], bank[:, m:n], u[:, col + m + 2:TX + 2], ALU.mult)
                    ins.then_inc(proj_dve, 1)
                    if j == 2:
                        dve.wait_ge(proj_dve, NX + i * 12 + 9)
                        dve.wait_ge(head_in, 16 * 5 * (i + 1))
                        link(dve.tensor_copy(u[:, META + SEQ:META + SEQ + 2], hist[:, :]))
                        dve.tensor_copy(ncp[:, bass.ds(i, 1), :].rearrange("p a c -> p (a c)"), u[:, META + SEQ - 2:META + SEQ])
                        dve.tensor_copy(ncs[:, bass.ds(i, 1), :].rearrange("p a c -> p (a c)"), u[:, TX:TX + 2])
                        parts = [(0, SEQ, META - 2), (SEQ, SAMPLE, META + SEQ)]
                        for a, w, s in parts:
                            ins = dve.tensor_scalar(y[:, a:a + w], u[:, s:s + w], cw[:, 0:1], None, ALU.mult)
                        link(ins)
                        for tap in (1, 2):
                            for a, w, s in parts:
                                ins = dve.scalar_tensor_tensor(y[:, a:a + w], u[:, s + tap:s + tap + w], cw[:, tap:tap + 1],
                                                               y[:, a:a + w], ALU.mult, ALU.add)
                            link(ins)
                else:
                    a = col - META
                    dve.tensor_tensor(y[:, a:a + n], bank[:, 0:n], y[:, a:a + n], ALU.mult).then_inc(proj_dve, 1)
                    dve.wait_ge(mix_hi_ready, i * 6 + 3 + j + 1)
                    sl = (slice(None), bass.ds(i, 1), slice(a, a + n))
                    dve.tensor_tensor(mid_lo[sl].rearrange("p a c -> p (a c)"), y[:, a:a + n],
                                      mid_hi[sl].rearrange("p a c -> p (a c)").bitcast(F32), ALU.subtract).then_inc(mix_ready, 1)

            def take_step(i, name):
                bank = ps[RET[STEPS.index(name) % 2]]
                dve.wait_ge(ret_done, i * NS + n_step(name))
                if name == "UC":
                    dve.wait_ge(head_in, 16 * 5 * (i + 1))
                    dve.wait_ge(s_new_out, 1 + 16 * i)
                    dve.tensor_copy(st[:, 0, :], bank[:, 0:HD])
                    dve.scalar_tensor_tensor(s_new[:, :], s_in[:, :], hc[:, C_G64:C_G64 + 1], bank[:, HD:2 * HD],
                                             ALU.mult, ALU.add).then_inc(ret_dve, 1)
                elif name in ("UA", "UB"):
                    if name == "UA":
                        dve.wait_ge(s_end_out, 1 + 16 * i)
                    c0 = 0 if name == "UA" else 4
                    for c in range(c0, c0 + 4):
                        ins = dve.scalar_tensor_tensor(st[:, (c + 1) % 5, :], st[:, c % 5, :], hc[:, C_G128:C_G128 + 1],
                                                       bank[:, (c - c0) * HD:(c - c0 + 1) * HD], ALU.mult, ALU.add)
                        if c < c0 + 3:
                            link(ins)
                    ins.then_inc(ret_dve, 1)
                elif name == "sC":
                    dve.tensor_tensor(smC[0:SAMPLE, :], bank[0:SAMPLE, 0:SAMPLE], hc[0:SAMPLE, 0:SAMPLE], ALU.mult).then_inc(ret_dve, 1)
                elif name in ("sA", "sB"):
                    mask = hc[:, 0:P].rearrange("p (a j) -> p a j", a=1).broadcast_to([P, 4, P])
                    dve.tensor_tensor(sm[:, :, :], bank[:, :].rearrange("p (c j) -> p c j", c=4), mask, ALU.mult).then_inc(ret_dve, 1)
                elif name in ("oC", "oA", "oB"):
                    w, n = (1, SAMPLE) if name == "oC" else (4, P)
                    for c in range(w):
                        ins = dve.bn_stats(bn[0:n, c, :], bank[0:n, c * HD:(c + 1) * HD])
                    link(ins)
                    m_even, s_even, m_odd, s_odd = (bn[0:n, 0:w, x] for x in (1, 2, 4, 5))
                    mean, diff, tot = (gs[0:n, x, 0:w] for x in range(3))
                    dve.tensor_tensor(mean, m_even, m_odd, ALU.add)
                    dve.tensor_tensor(diff, m_even, m_odd, ALU.subtract)
                    link(dve.tensor_tensor(tot, s_even, s_odd, ALU.add))
                    dve.tensor_scalar(mean, mean, 0.5, None, ALU.mult)
                    link(dve.scalar_tensor_tensor(diff, diff, 0.25, diff, ALU.mult, ALU.mult))
                    link(dve.scalar_tensor_tensor(tot, tot, 1.0 / HD, diff, ALU.mult, ALU.add))
                    ins = dve.tensor_scalar(small[0:n, 0, 0:w], tot, hc[0:n, C_C2:C_C2 + 1], GN_EPS, ALU.mult, ALU.add)
                    ins.then_inc(var_ready, 1)
                    dve.wait_ge(gsd_ready, i * 3 + ["oC", "oA", "oB"].index(name) + 1)
                    link(dve.reciprocal(small[0:n, 2, 0:w], small[0:n, 1, 0:w]))
                    link(dve.tensor_scalar(small[0:n, 3, 0:w], small[0:n, 2, 0:w], hc[0:n, C_C:C_C + 1], None, ALU.mult))
                    for c in range(w):
                        dst = onC[0:n, :] if name == "oC" else on[:, c, :]
                        ins = dve.tensor_scalar(dst, bank[0:n, c * HD:(c + 1) * HD], gs[0:n, 0, c:c + 1], small[0:n, 3, c:c + 1],
                                                ALU.subtract, ALU.mult)
                    ins.then_inc(ret_dve, 1)
                elif name in ("tC", "tA", "tB"):
                    dve.wait_ge(proj_act, i * 9 + 6)
                    col, n = {"tC": (SEQ, SAMPLE), "tA": (0, 512), "tB": (512, 512)}[name]
                    og = onC[:, 0:SAMPLE] if name == "tC" else on[:, :, :].rearrange("p c e -> p (c e)")
                    dve.scalar_tensor_tensor(og, bank[:, 0:n], gnw[:, 0:1], vg[:, META + col:META + col + n],
                                             ALU.mult, ALU.mult).then_inc(ret_dve, 1)
                    dve.wait_ge(mix_hi_ready, i * 6 + MIX_PARTS.index(name) + 1)
                    sl = (slice(None), bass.ds(i + 4, 1), slice(col, col + n))
                    dve.tensor_tensor(mid_lo[sl].rearrange("p a c -> p (a c)"), og,
                                      mid_hi[sl].rearrange("p a c -> p (a c)").bitcast(F32), ALU.subtract).then_inc(mix_ready, 1)

            LINKS = 34

            def iteration(i, last):
                before = chain["n"]
                for un in range(NU):
                    for b in range(6):
                        half = 2 * un + b // 3
                        if b % 3 == 0 and half >= 1 and not (last and half + 1 == HALVES):
                            split_in(i, half + 1)
                        if b >= 3 and names[un] in DVE_UNITS:
                            take_unit(i, names[un], b - 3)
                        if (un, b) in AFTER and AFTER[un, b] in BY_DVE:
                            take_step(i, AFTER[un, b])
                if not last:
                    split_in(i, HALVES + 1)
                assert chain["n"] - before == LINKS, chain["n"] - before

            start = chain["n"]
            with dve.Fori(0, HEADS - 1) as i:
                chain["base"] = i * LINKS
                iteration(i, False)
            chain.update(n=start + (HEADS - 1) * LINKS, base=0)
            iteration(HEADS - 1, True)

            for m in range(2 * KT):
                dve.wait_ge(w_hi, H_OUT + m + 1)
                s, _ = raw_slot(H_OUT + m)
                sl = (slice(None), KORDER[m // 2], slice(m % 2 * 512, m % 2 * 512 + 512))
                dve.tensor_tensor(wo_lo[sl], raw[:, s, :], wo_hi[sl].bitcast(F32), ALU.subtract).then_inc(w_split, 1)
            dve.wait_ge(normw_in, 16)

            def residual(t):
                n = rows(t)
                dve.wait_ge(out_done, t + 1)
                if t == 0:
                    dve.wait_ge(h_in, 16)
                if t == 2:
                    dve.wait_ge(h_rest_in, 32)
                pair = PAIRS3[t if t < 2 else (2 * t - 1) % 4]
                for nh in range(2):
                    sl = slice(nh * 512, nh * 512 + 512)
                    ins = dve.tensor_tensor(h[0:n, t, sl], ps[pair[nh]][0:n, :], h[0:n, t, sl], ALU.add)
                ins.then_inc(out_taken, 1)
                dve.wait_ge(out_taken, t + 1)
                if t >= 2:
                    dve.wait_ge(ht_done, t - 1)
                dve.tensor_tensor(hw[0:n, t % 2, :], h[0:n, t, :], normw[0:n, :], ALU.mult).then_inc(hw_ready, 1)
                link(mean_square(h[0:n, t, :], n, 0))
                dve.reciprocal(inv_ms[0:n, t:t + 1], small[0:n, 0, 0:1]).then_inc(ms2_ready, 1)

            def ht_lo(t):
                n = rows(t)
                dve.wait_ge(ht_hi_ready, t + 1)
                for b in range(2):
                    sl = (slice(None), slice(4 * b, 4 * b + 4), slice(t * P, t * P + n))
                    last = dve.tensor_tensor(mid_lo[sl], ps[PAIRS3[(2 * t + 2) % 4][b]][:, 0:4 * n].rearrange("p (k c) -> p k c", k=4),
                                             mid_hi[sl].bitcast(F32), ALU.subtract)
                last.then_inc(ht_ready, 1)

            def split_ffn(g, kind, a, half):
                n = ffn_half(kind, a, half)
                s, _ = raw_slot(n)
                dve.wait_ge(w_hi, n + 1 + g * NF)
                if kind == "wd":
                    sl = (slice(None), a, slice(half * 512, half * 512 + 512))
                    dve.tensor_tensor(wd_lo[sl], raw[:, s, :], wd_hi[sl].bitcast(F32), ALU.subtract).then_inc(w_split, 1)
                else:
                    dve.tensor_tensor(ws_lo[:, half], raw[:, s, :].rearrange("p (k c) -> p k c", k=4),
                                      ws_hi[:, half].bitcast(F32), ALU.subtract).then_inc(w_split, 1)

            residual(0)
            residual(1)
            ht_lo(0)
            for t in range(2, TILES):
                residual(t)
                ht_lo(t - 1)
                if t == 3:
                    split_ffn(0, "up", 0, 0)
                    split_ffn(0, "up", 0, 1)
            ht_lo(TILES - 1)

            def take_down(g, t):
                n = rows(t)
                dve.wait_ge(down_done, 9 * g + t + 1)
                pair = DOWN_PAIRS[t % 3]
                for nh in range(2):
                    sl = slice(nh * 512, nh * 512 + 512)
                    ins = dve.scalar_tensor_tensor(h[0:n, t, sl], ps[pair[nh]][0:n, :], inv_ms[0:n, t:t + 1], h[0:n, t, sl],
                                                   ALU.mult, ALU.add)
                ins.then_inc(down_taken, 1)

            def group(g, last):
                for p in range(8):
                    if 1 <= p:
                        split_ffn(g, *FFN_ORDER[2 * p - 2])
                        split_ffn(g, *FFN_ORDER[2 * p - 1])
                    if p % 2 == 1:
                        a = p // 2
                        for j in range(3):
                            n = 3 * a + j
                            w = CGY[j][1]
                            sl = (slice(None), a, slice(CGY[j][0], CGY[j][0] + w))
                            dve.wait_ge(relu_done, 12 * g + n + 1)
                            dve.tensor_tensor(sq[:, n % 2, 0:w], rl[:, n % 2, 0:w], rl[:, n % 2, 0:w], ALU.mult).then_inc(sq_done, 1)
                            dve.wait_ge(f_hi_ready, 12 * g + n + 1)
                            dve.tensor_tensor(f_lo[sl], sq[:, n % 2, 0:w], f_hi[sl].bitcast(F32), ALU.subtract).then_inc(f_ready, 1)
                if not last:
                    split_ffn(g, "next", 0, 0)
                    split_ffn(g, "next", 0, 1)
                for t in range(TILES):
                    take_down(g, t)
                    if last:
                        n = rows(t)
                        dve.wait_ge(down_taken, 2 + 9 * g + t + 1)
                        mean_square(h[0:n, t, :], n, t % 4).then_inc(fin_ms, 1)
                        dve.wait_ge(fin_sd, t + 1)
                        link(dve.reciprocal(small[0:n, t % 4, 2:3], small[0:n, t % 4, 1:2]))
                        if t >= 2:
                            dve.wait_ge(y_out[t % 2], 16 * (t // 2))
                        dve.scalar_tensor_tensor(hw[0:n, t % 2, :], h[0:n, t, :], small[0:n, t % 4, 2:3], normw[0:n, :],
                                                 ALU.mult, ALU.mult).then_inc(y_ready, 1)

            with dve.Fori(0, GROUPS - 1) as g:
                group(g, False)
            dve.wait_ge(normw_in, 32)
            group(GROUPS - 1, True)

        @block.tensor
        def _(pe):
            def passes(out, a_hi, a_lo, b_hi, b_lo, start, stop):
                pe.matmul(out, a_hi, b_hi, start=start, stop=False)
                pe.matmul(out, a_lo, b_hi, start=False, stop=False)
                return pe.matmul(out, a_hi, b_lo, start=False, stop=stop)

            for t in range(XTILES):
                n = xrows(t)
                pe.wait_ge(xn_ready, t + 1)
                if t >= 2:
                    pe.wait_ge(hn_ready, t - 1)
                for k in range(KT):
                    last = pe.transpose(ps[T_PAIRS[t % 2][k // 4]][:, k % 4 * n:k % 4 * n + n],
                                        xr[0:n, t % 4, k * P:(k + 1) * P], ident[0:n, 0:n])
                last.then_inc(xt_done, 1)

            names = [x[0] for x in UNITS]

            def bank_free(i, un, j):
                name = names[un]
                if name == "v":
                    pe.wait_ge(proj_dve, i * 12 + j + 1)
                elif name == "q":
                    pe.wait_ge(proj_act, i * 9 + j + 1)
                elif name == "g":
                    pe.wait_ge(proj_dve, NX + i * 12 + j + 1)
                elif name == "xt":
                    pe.wait_ge(proj_dve, NX + i * 12 + 3 + j + 1)
                elif name == "c":
                    pe.wait_ge(proj_act, i * 9 + 3 + j + 1)
                elif name == "b":
                    pe.wait_ge(proj_act, i * 9 + 6 + j + 1)

            def step(i, name):
                s = STEPS.index(name)
                out = ps[RET[s % 2]]
                if s < 2:
                    pe.wait_ge(proj_dve, NX + i * 12)
                elif STEPS[s - 2] in BY_ACT:
                    pe.wait_ge(ret_act, i * len(BY_ACT) + n_act(STEPS[s - 2]))
                else:
                    pe.wait_ge(ret_dve, i * len(BY_DVE) + n_dve(STEPS[s - 2]))
                c0 = 4 if name[1] == "B" else 0
                if name[0] in "vk" and name[1] in "AB":
                    src = vg if name[0] == "v" else kT
                    if name[0] == "v":
                        pe.wait_ge(proj_act, i * 9 + (2 if name == "vA" else 3))
                    for c in range(4):
                        at = META + (c0 + c) * P
                        last = pe.transpose(out[:, c * P:(c + 1) * P], src[:, at:at + P], ident[:, :])
                elif name in ("vC", "kC"):
                    src = vg if name == "vC" else kT
                    if name == "kC":
                        pe.wait_ge(proj_dve, NX + i * 12 + 3)
                    pe.transpose(out[0:META, 0:HD], src[:, 0:META], ident[:, :])
                    last = pe.transpose(out[0:SAMPLE, HD:2 * HD], src[:, META + SEQ:TX], ident[:, :])
                elif name == "UC":
                    pe.wait_ge(ret_act, i * len(BY_ACT) + n_act("kC"))
                    pe.matmul(out[:, 0:HD], kdC[0:META, 0, :], v_tok[0:META, 8, :], start=True, stop=True)
                    last = pe.matmul(out[:, HD:2 * HD], kdC[0:SAMPLE, 1, :], v_tok[0:SAMPLE, 9, :], start=True, stop=True)
                elif name in ("UA", "UB"):
                    pe.wait_ge(ret_act, i * len(BY_ACT) + n_act("kA" if name == "UA" else "kB"))
                    for c in range(4):
                        last = pe.matmul(out[:, c * HD:(c + 1) * HD], kd[:, c, :], v_tok[:, c0 + c, :], start=True, stop=True)
                elif name == "sC":
                    pe.wait_ge(proj_dve, NX + i * 12 + 6)
                    last = pe.matmul(out[0:SAMPLE, 0:SAMPLE], kT[:, META + SEQ:TX], qT[:, SEQ:TY], start=True, stop=True)
                elif name in ("sA", "sB"):
                    for c in range(4):
                        at = (c0 + c) * P
                        last = pe.matmul(out[:, c * P:(c + 1) * P], kT[:, META + at:META + at + P], qT[:, at:at + P], start=True, stop=True)
                elif name == "oC":
                    pe.wait_ge(ret_dve, i * len(BY_DVE) + n_dve("sC"))
                    pe.wait_ge(head_in, 16 * 5 * (i + 1))
                    pe.matmul(out[0:SAMPLE, 0:HD], qT[:, SEQ:TY], s_in[:, :], start=True, stop=False)
                    last = pe.matmul(out[0:SAMPLE, 0:HD], smC[0:SAMPLE, :], v_tok[0:SAMPLE, 9, :], start=False, stop=True)
                elif name in ("oA", "oB"):
                    pe.wait_ge(ret_dve, i * len(BY_DVE) + n_dve("sA" if name == "oA" else "sB"))
                    for c in range(4):
                        at = (c0 + c) * P
                        pe.matmul(out[:, c * HD:(c + 1) * HD], sm[:, c, :], v_tok[:, c0 + c, :], start=True, stop=False)
                        last = pe.matmul(out[:, c * HD:(c + 1) * HD], qT[:, at:at + P], st[:, (c0 + c) % 5, :], start=False, stop=True)
                elif name == "tC":
                    last = pe.transpose(out[:, 0:P], onC[:, :], ident[:, :])
                else:
                    pe.wait_ge(ret_dve, i * len(BY_DVE) + n_dve("oA" if name == "tA" else "oB"))
                    for c in range(4):
                        last = pe.transpose(out[:, c * P:(c + 1) * P], on[:, c, :], ident[:, :])
                last.then_inc(ret_done, 1)

            def iteration(i):
                for un, (_, _, groups) in enumerate(UNITS):
                    for half in range(2):
                        n = 2 * un + half
                        pe.wait_ge(w_split, i * HALVES + n + 1)
                        for j, (col, w) in enumerate(groups):
                            if un == 0 and half == 0:
                                pe.wait_ge(hn_ready, (XTILES // 3) * (j + 1))
                            if half == 0:
                                bank_free(i, un, j)
                            out = ps[un % 2 * 3 + j][:, 0:w]
                            for k in range(4):
                                kk = 4 * half + k
                                last = passes(out, ws_hi[:, n % 2, k, :], ws_lo[:, n % 2, k, :],
                                              hn_hi[:, kk, col:col + w], hn_lo[:, kk, col:col + w],
                                              start=kk == 0, stop=kk == KT - 1)
                            if half == 1:
                                last.then_inc(proj_done, 1)
                            if (un, 3 * half + j) in AFTER and j < 2:
                                step(i, AFTER[un, 3 * half + j])
                        if half == 0:
                            last.then_inc(w_used, 1)
                        if (un, 3 * half + 2) in AFTER:
                            step(i, AFTER[un, 3 * half + 2])
            with pe.Fori(0, HEADS) as i:
                iteration(i)

            def out_pair(t):
                return PAIRS3[t if t < 2 else (2 * t - 1) % 4]

            def out_part(t, i, k):
                n = rows(t)
                for nh in range(2):
                    sl = slice(nh * 512, nh * 512 + 512)
                    last = passes(ps[out_pair(t)[nh]][0:n, :], mid_hi[:, k, t * P:t * P + n], mid_lo[:, k, t * P:t * P + n],
                                  wo_hi[:, k, sl], wo_lo[:, k, sl], start=i == 0, stop=i == KT - 1)
                return last

            def transposed(t):
                n = rows(t)
                pe.wait_ge(hw_ready, t + 1)
                if t == 1:
                    pe.wait_ge(out_taken, 1)
                elif t >= 2:
                    pe.wait_ge(ht_ready, t - 1)
                for k in range(KT):
                    last = pe.transpose(ps[PAIRS3[(2 * t + 2) % 4][k // 4]][:, k % 4 * n:k % 4 * n + n],
                                        hw[0:n, t % 2, k * P:(k + 1) * P], ident[0:n, 0:n])
                last.then_inc(ht_done, 1)

            pe.wait_ge(ret_dve, len(BY_DVE) * HEADS)
            for i, k in enumerate(KORDER):
                pe.wait_ge(w_split, H_OUT + 2 * i + 2)
                pe.wait_ge(mix_ready, len(MIX_PARTS) * HEADS - (3 if k >= 4 else 0))
                for t in range(2):
                    last = out_part(t, i, k)
                    if i == KT - 1:
                        last.then_inc(out_done, 1)
            for t in range(2, TILES):
                if t == 2:
                    pe.wait_ge(proj_dve, NX + 12 * HEADS)
                else:
                    pe.wait_ge(out_taken, t - 1)
                for i, k in enumerate(KORDER):
                    last = out_part(t, i, k)
                last.then_inc(out_done, 1)
                transposed(t - 2)
            transposed(TILES - 2)
            transposed(TILES - 1)

            def group(g, first):
                for a in range(FT):
                    for half in range(2):
                        slot = half
                        if a == 0:
                            pe.wait_ge(w_split, H_FFN + half + 1 + g * NF)
                        else:
                            pe.wait_ge(w_split, ffn_half("up", a, half) + 1 + g * NF)
                        for j, (col, w) in enumerate(CGY):
                            if half == 0:
                                if first and a == 0:
                                    pe.wait_ge(ht_ready, [3, 6, 9][j])
                                    if j == 0:
                                        pe.wait_ge(ht_ready, TILES)
                                elif a == 0:
                                    pe.wait_ge(down_taken, 9 * g + (0 if j < 2 else 1))
                                elif a == 1:
                                    if not first:
                                        pe.wait_ge(relu_done, 12 * g)
                                        pe.wait_ge(down_taken, 9 * g + 1)
                                else:
                                    pe.wait_ge(relu_done, 12 * g + 3 * (a - 2) + j + 1)
                            out = ps[a % 2 * 3 + j][:, 0:w]
                            for k in range(4):
                                kk = 4 * half + k
                                last = passes(out, ws_hi[:, slot, k, :], ws_lo[:, slot, k, :],
                                              mid_hi[:, kk, col:col + w], mid_lo[:, kk, col:col + w],
                                              start=kk == 0, stop=kk == KT - 1)
                            if half == 1:
                                last.then_inc(up_done, 1)
                        if half == 0:
                            last.then_inc(w_used, 1)
                for t in range(TILES):
                    n = rows(t)
                    if t == 0:
                        pe.wait_ge(w_split, ffn_half("wd", 3, 1) + 1 + g * NF)
                    pe.wait_ge(f_ready, 12 * g + 9 + 1 + (t * P + n - 1) // BLK)
                    if t == 1:
                        pe.wait_ge(relu_done, 12 * g + 10)
                    elif t == 2:
                        pe.wait_ge(down_taken, 2 + 9 * g)
                    elif t >= 3:
                        pe.wait_ge(down_taken, 2 + 9 * g + t - 2)
                    for nh in range(2):
                        sl = slice(nh * 512, nh * 512 + 512)
                        for a in range(FT):
                            last = passes(ps[DOWN_PAIRS[t % 3][nh]][0:n, :], f_hi[:, a, t * P:t * P + n],
                                          f_lo[:, a, t * P:t * P + n], wd_hi[:, a, sl], wd_lo[:, a, sl],
                                          start=a == 0, stop=a == FT - 1)
                    last.then_inc(down_done, 1)

            group(0, True)
            with pe.Fori(1, GROUPS) as g:
                group(g, False)


_INS = ["x_prompt", "x_sample", "state_conv", "state_ret", "meta_tokens", "norm_mix_w", "w_in", "conv_w", "ret_gn_w",
        "w_out", "norm_ffn_w", "w_up", "w_down", "norm_final_w"]
_OUTS = [(1, SEQ, D), (1, SAMPLE, D), (1, 1, 2, DC), (1, 1, HEADS, HD, HD), (1, 1, 2, DC), (1, 1, HEADS, HD, HD)]


def kernel(**inputs):
    import concourse.bacc as bacc
    from concourse.bass_utils import run_bass_kernel_spmd

    nc = bacc.Bacc("TRN2", target_bir_lowering=False, num_devices=1)
    arrays, args = {}, []
    for name, a in [(n, np.ascontiguousarray(inputs[n])) for n in _INS] + list(constants().items()):
        arrays[f"in_{name}"] = a
        args.append(nc.dram_tensor(f"in_{name}", a.shape, mybir.dt.from_np(a.dtype), kind="ExternalInput").ap())
    for i, shape in enumerate(_OUTS):
        args.append(nc.dram_tensor(f"out_{i}", shape, F32, kind="ExternalOutput").ap())
    build(nc, *args)
    r = run_bass_kernel_spmd(nc, [arrays], core_ids=[0])
    return tuple(r.results[0][f"out_{i}"] for i in range(len(_OUTS)))
```

```python
from contextlib import ExitStack

import numpy as np

import concourse.bass as bass
from concourse import mybir

F32 = mybir.dt.float32
F32R = mybir.dt.float32r
ALU = mybir.AluOpType
ACT = mybir.ActivationFunctionType

P = 128
D = 1024
SEQ = 1024
SAMPLE = 64
PAST = 256
META = 16
DC = 512
HEADS = 4
HD = 128
FF = 4 * D
DIN = 3 * DC + 4 * HEADS * HD
EPS = 1e-6
GN_EPS = 1e-5

KT = D // P
TX = META + SEQ + SAMPLE
TY = SEQ + SAMPLE
TILES = (TY + P - 1) // P
XTILES = (TX + P - 1) // P
BLK = 368
CGX = [(0, 368), (368, 368), (736, 368)]
CGQ = [(16, 352), (368, 368), (736, 368)]
CGY = [(0, 368), (368, 368), (736, 352)]

CONV = [(0, SEQ, META - 2), (SEQ, SAMPLE, META + SEQ)]
UNITS = [("v", 3 * DC + 2 * DC, CGX), ("k", 3 * DC + DC, CGX), ("q", 3 * DC, CGQ),
         ("g", 3 * DC + 3 * DC, CGQ), ("xt", 0, CGX), ("c", 2 * DC, CGX), ("b", DC, CGQ)]
NU = len(UNITS)
HALVES = 2 * NU
STEPS = ["vA", "vB", "vC", "kC", "UC", "kA", "UA", "sC", "sA", "oC", "oA", "kB", "UB", "tC", "tA",
         "sB", "oB", "tB"]
FIRST = {"vA": (2, 0), "vB": (2, 1), "vC": (2, 2), "kC": (2, 3), "UC": (2, 4), "kA": (2, 5), "UA": (3, 0)}
AFTER = {(1, 1): "vA", (1, 2): "vB", (1, 3): "vC", (2, 2): "kC", (2, 3): "UC", (2, 4): "kA",
         (2, 5): "UA", (3, 2): "sC", (3, 3): "sA", (3, 4): "oC", (3, 5): "oA", (4, 0): "kB",
         (4, 1): "UB", (4, 2): "tC", (4, 3): "tA", (4, 4): "sB", (5, 1): "oB", (5, 5): "tB"}
NS = len(STEPS)
AFTER_FIRST = {**{at: s for at, s in AFTER.items() if s not in FIRST}, **{at: s for s, at in FIRST.items()}}
BY_ACT = ["vA", "vB", "vC", "kC", "kA", "kB"]
BY_DVE = [s for s in STEPS if s not in BY_ACT]
ACT_UNITS = ["v", "g", "xt"]
DVE_UNITS = ["k", "q", "c", "b"]
MIX_PARTS = ["tC", "tA", "tB", 0, 1, 2]
KORDER = [4, 5, 6, 7, 0, 1, 2, 3]
GROUPS = 8
FT = FF // GROUPS // P
C_MASK, C_KDEC, C_KMETA, C_KSAMP, C_C, C_C2, C_G128, C_G64, NCONST = 0, 128, 129, 130, 131, 132, 133, 134, 135


def constants():
    half = HD // 2
    inv = (np.float32(10000.0) ** (-np.arange(half, dtype=np.float32) / np.float32(half))).astype(np.float32)
    pos = np.concatenate([np.arange(META + SEQ) - META, np.arange(SAMPLE) + PAST]).astype(np.float32)
    ang = (pos[None, :] * inv[:, None]).astype(np.float32).astype(np.float64)
    cos = np.concatenate([np.cos(ang), np.cos(ang)]).astype(np.float32)
    sin = np.concatenate([-np.sin(ang), np.sin(ang)]).astype(np.float32)
    head = np.zeros((HEADS, P, NCONST), np.float64)
    j = np.arange(P)
    scale = HD ** -0.5
    for h in range(HEADS):
        lg = np.log(1.0 - 2.0 ** (-5.0 - h))
        head[h, :, :P] = np.where(j[None, :] >= j[:, None], np.exp(-(j[:, None] + 1) * lg), 0.0) * scale
        head[h, :, C_KDEC] = np.exp((P - 1 - j) * lg) * scale
        head[h, :META, C_KMETA] = np.exp((META - 1 - j[:META]) * lg) * scale
        head[h, :SAMPLE, C_KSAMP] = np.exp((SAMPLE - 1 - j[:SAMPLE]) * lg) * scale
        head[h, :, C_C] = np.exp((j + 1) * lg)
        head[h, :, C_C2] = np.exp(2 * (j + 1) * lg)
        head[h, :, C_G128] = np.exp(P * lg)
        head[h, :, C_G64] = np.exp(SAMPLE * lg)
    return {"c_cos": cos, "c_sin": sin, "c_head": head.astype(np.float32), "c_ident": np.eye(P, dtype=np.float32)}


def build(nc, x_prompt, x_sample, state_conv, state_ret, meta_tokens, norm_mix_w, w_in, conv_w, ret_gn_w,
          w_out, norm_ffn_w, w_up, w_down, norm_final_w, c_cos, c_sin, c_head, c_ident,
          y_prompt, y_sample, new_conv_prompt, new_ret_prompt, new_conv_sample, new_ret_sample):
    ctx = ExitStack()
    with ctx:
        base = (nc.sbuf_base + 31) // 32 * 32
        place = {"at": base}

        def region(size):
            at = place["at"]
            place["at"] = at + (size + 31) // 32 * 32
            return at

        def sb(name, shape, at, dt=F32):
            return nc.alloc_sbuf_tensor_at(name, shape, dt, offset=at)

        r1 = region(2 * KT * TX * 4)
        hn_hi = sb("hn_hi", [P, KT, TX], r1, F32R)
        hn_lo = sb("hn_lo", [P, KT, TX], r1 + KT * TX * 4, F32R)
        wo_hi = sb("wo_hi", [P, KT, D], r1, F32R)
        wo_lo = sb("wo_lo", [P, KT, D], r1 + KT * TX * 4, F32R)
        f_hi = sb("f_hi", [P, FT, TY], r1, F32R)
        f_lo = sb("f_lo", [P, FT, TY], r1 + FT * TY * 4, F32R)
        wd_hi = sb("wd_hi", [P, FT, D], r1 + 2 * FT * TY * 4, F32R)
        wd_lo = sb("wd_lo", [P, FT, D], r1 + 2 * FT * TY * 4 + FT * D * 4, F32R)
        r2 = region(2 * KT * TY * 4)
        xr = sb("xr", [P, 4, D], r2)
        mid_hi = sb("mid_hi", [P, KT, TY], r2, F32R)
        mid_lo = sb("mid_lo", [P, KT, TY], r2 + KT * TY * 4, F32R)
        ws_hi = sb("ws_hi", [P, 2, 4, P], region(4096), F32R)
        ws_lo = sb("ws_lo", [P, 2, 4, P], region(4096), F32R)
        raw = sb("raw", [P, 4, 512], region(8192))
        normw = sb("normw", [P, D], region(4096))
        ident = sb("ident", [P, P], region(512))
        bn = sb("bn", [P, 4, 6], region(96))
        mv = sb("mv", [P, 2], region(8))
        gs = sb("gs", [P, 3, 4], region(48))
        small = sb("small", [P, 4, 4], region(64))
        inv_ms = sb("inv_ms", [P, TILES], region(36))
        eps = sb("eps", [P, 1], region(4))
        r3 = place["at"]

        v_tok = sb("v_tok", [P, 10, HD], region(10 * HD * 4))
        u = sb("u", [P, TX + 2], region((TX + 2) * 4))
        y = sb("y", [P, TY], region(TY * 4))
        cos_t = sb("cos_t", [P, TX], region(TX * 4))
        sin_t = sb("sin_t", [P, TX], region(TX * 4))
        qT = sb("qT", [P, TY], region(TY * 4))
        kT = sb("kT", [P, TX], region(TX * 4))
        vg = sb("vg", [P, TX], region(TX * 4))
        sm = sb("sm", [P, 4, P], region(2048))
        kd = sb("kd", [P, 4, HD], region(2048))
        on = sb("on", [P, 4, HD], region(2048))
        st = sb("st", [P, 5, HD], region(2560))
        smC = sb("smC", [P, SAMPLE], region(256))
        onC = sb("onC", [P, HD], region(512))
        kdC = sb("kdC", [P, 2, HD], region(1024))
        s_in = sb("s_in", [P, HD], region(512))
        s_new = sb("s_new", [P, HD], region(512))
        rot = sb("rot", [P, BLK], region(BLK * 4))
        hc = sb("hc", [P, NCONST], region(NCONST * 4))
        gnw = sb("gnw", [P, 1], region(4))
        cw = sb("cw", [P, 3], region(12))
        hist = sb("hist", [P, 2], region(8))
        ncp = sb("ncp", [P, HEADS, 2], region(32))
        ncs = sb("ncs", [P, HEADS, 2], region(32))
        end2 = place["at"]

        place["at"] = r3
        kx_hi = sb("kx_hi", [P, 2, 4, P], region(4096), F32R)
        kx_lo = sb("kx_lo", [P, 2, 4, P], region(4096), F32R)
        junk = sb("junk", [P, D], region(4096))

        place["at"] = r3
        h = sb("h", [P, TILES, D], region(TILES * D * 4))
        hw = sb("hw", [P, 2, D], region(2 * D * 4))
        rl = sb("rl", [P, 2, BLK], region(2 * BLK * 4))
        sq = sb("sq", [P, 2, BLK], region(2 * BLK * 4))
        assert max(end2, place["at"]) <= nc.sbuf_usable_end, (end2, place["at"], nc.sbuf_usable_end)

        ps = [ctx.enter_context(nc.psum_tensor(f"ps{n}", [P, 512], F32)) for n in range(8)]
        T_PAIRS = [(2, 5), (6, 7)]
        RET = [6, 7]
        PAIRS3 = [(4, 5), (6, 7), (0, 1), (2, 3)]
        def T3(t):
            return PAIRS3[(2 * t + 2) % 4 if t < TILES - 1 else 1]

        DOWN_PAIRS = [(0, 1), (2, 3), (6, 7)]

        def sem(name):
            return ctx.enter_context(nc.semaphore(name))

        eps_ready = sem("eps_ready")
        act_step = sem("act_step")
        const_in = sem("const_in")
        rope_in = sem("rope_in")
        x_in = [sem(f"x_in{n}") for n in range(4)]
        ss_ready = sem("ss_ready")
        sd_ready = sem("sd_ready")
        xn_ready = sem("xn_ready")
        xt_done = sem("xt_done")
        hn_hi_ready = sem("hn_hi_ready")
        hn_ready = sem("hn_ready")
        raw_in = [sem(f"raw_in{n}") for n in range(4)]
        w_hi = sem("w_hi")
        w_split = sem("w_split")
        w_used = sem("w_used")
        proj_done = sem("proj_done")
        proj_act = sem("proj_act")
        proj_dve = sem("proj_dve")
        ret_done = sem("ret_done")
        ret_act = sem("ret_act")
        ret_dve = sem("ret_dve")
        head_in = sem("head_in")
        var_ready = sem("var_ready")
        gsd_ready = sem("gsd_ready")
        mix_hi_ready = sem("mix_hi_ready")
        mix_ready = sem("mix_ready")
        s_new_out = sem("s_new_out")
        s_end_out = sem("s_end_out")
        conv_out = sem("conv_out")
        normw_in = sem("normw_in")
        h_in = sem("h_in")
        h_rest_in = sem("h_rest_in")
        out_done = sem("out_done")
        out_taken = sem("out_taken")
        hw_ready = sem("hw_ready")
        ht_done = sem("ht_done")
        ht_hi_ready = sem("ht_hi_ready")
        ht_ready = sem("ht_ready")
        ms2_ready = sem("ms2_ready")
        tap0_ready = sem("tap0_ready")
        up_done = sem("up_done")
        relu_done = sem("relu_done")
        sq_done = sem("sq_done")
        f_hi_ready = sem("f_hi_ready")
        f_ready = sem("f_ready")
        down_done = sem("down_done")
        down_taken = sem("down_taken")
        fin_ms = sem("fin_ms")
        fin_sd = sem("fin_sd")
        y_ready = sem("y_ready")
        y_out = [sem("y_out0"), sem("y_out1")]
        dve_step = sem("dve_step")
        NX = 3

        w_in_t = w_in[0].rearrange("(k p) n -> p k n", p=P)
        w_up_t = w_up[0].rearrange("(k p) n -> p k n", p=P)
        w_out_t = w_out[0].rearrange("(k p) n -> p k n", p=P)
        w_down_t = w_down[0].rearrange("(k p) n -> p k n", p=P)
        meta_d, xp_d, xs_d = meta_tokens, x_prompt[0], x_sample[0]

        def x_rows(t):
            lo, hi = t * P, min((t + 1) * P, TX)
            out = []
            for src, a, b in ((meta_d, 0, META), (xp_d, META, META + SEQ), (xs_d, META + SEQ, TX)):
                s, e = max(lo, a), min(hi, b)
                if s < e:
                    out.append((src[s - a:e - a, :], s - lo, e - s))
            return out

        def rows(t):
            return min(P, TY - t * P)

        def xrows(t):
            return min(P, TX - t * P)

        X_COUNT = []
        seen = [0] * 4
        for t in range(XTILES):
            seen[t % 4] += 16 * len(x_rows(t))
            X_COUNT.append(seen[t % 4])

        def n_step(name):
            return STEPS.index(name) + 1

        def n_act(name):
            return BY_ACT.index(name) + 1

        def n_dve(name):
            return BY_DVE.index(name) + 1

        H_OUT = HALVES * HEADS
        H_FFN = H_OUT + 2 * KT
        FFN_ORDER = []
        for p in range(1, 7):
            FFN_ORDER += [("wd", (p - 1) // 2, (p - 1) % 2), ("up", (p + 1) // 2, (p + 1) % 2)]
        FFN_ORDER += [("wd", 3, 0), ("wd", 3, 1), ("next", 0, 0), ("next", 0, 1)]
        NF = len(FFN_ORDER)
        assert NF == 4 * FT

        def ffn_half(kind, a, half):
            return H_FFN + 2 + FFN_ORDER.index((kind, a, half)) if (kind, a) != ("up", 0) else H_FFN + half

        def raw_slot(n):
            m = n - H_OUT
            s = (m + 2) % 4
            return s, m // 4 + (H_OUT // 2 - 1 if s < 2 else 1)

        def raw_before(i):
            return i * NU - (0 if isinstance(i, int) and i == 0 else 1)

        block = ctx.enter_context(nc.Block())

        @block.sync
        def _(sp):
            def load_x(t):
                if t >= 4:
                    sp.wait_ge(xt_done, t - 3)
                for src, at, n in x_rows(t):
                    sp.dma_start(xr[at:at + n, t % 4, :], src).then_inc(x_in[t % 4], 16)

            def load_in(i, n, slot=None):
                off = UNITS[n // 2][1] + i * P
                s = n % 2 if slot is None else slot
                sp.dma_start(raw[:, s, :].rearrange("p (k c) -> p k c", k=4),
                             w_in_t[:, 4 * (n % 2):4 * (n % 2) + 4, bass.ds(off, P)]).then_inc(raw_in[s], 16)

            def iteration(i, first):
                for n in range(HALVES):
                    if not (first and n < 4):
                        sp.wait_ge(w_split, i * HALVES + n - 1)
                        load_in(i, n)
                    if n == 3:
                        sp.wait_ge(proj_dve, NX + i * 12)
                        sp.dma_start(hc[:, :], c_head[bass.ds(i, 1), :, :].rearrange("a p c -> p (a c)")).then_inc(head_in, 16)
                        sp.dma_start(s_in[:, :], state_ret[0, 0, bass.ds(i, 1), :, :].rearrange("a p c -> p (a c)")).then_inc(head_in, 16)
                        sp.dma_start(gnw[:, :], ret_gn_w[0:1, bass.ds(i * P, P)].rearrange("a p -> p a")).then_inc(head_in, 16)
                        sp.dma_start(cw[:, :], conv_w[0, :, bass.ds(i * P, P)].rearrange("w p -> p w"), allow_slow_non_contiguous=True).then_inc(head_in, 16)
                        sp.dma_start(hist[:, :], state_conv[0, 0, :, bass.ds(i * P, P)].rearrange("w p -> p w"), allow_slow_non_contiguous=True).then_inc(head_in, 16)
                    if n == 9:
                        sp.wait_ge(ret_dve, i * len(BY_DVE) + n_dve("UC"))
                        sp.dma_start(new_ret_sample[0, 0, bass.ds(i, 1), :, :].rearrange("a p c -> p (a c)"), s_new[:, :]).then_inc(s_new_out, 16)
                    if n == 12:
                        sp.wait_ge(ret_dve, i * len(BY_DVE) + n_dve("UB"))
                        sp.dma_start(new_ret_prompt[0, 0, bass.ds(i, 1), :, :].rearrange("a p c -> p (a c)"), st[:, 8 % 5, :]).then_inc(s_end_out, 16)

            load_x(0)
            sp.dma_start(normw[:, :], norm_mix_w[0:1, :].broadcast_to([P, D])).then_inc(const_in, 16)
            sp.dma_start(ident[:, :], c_ident).then_inc(const_in, 16)
            load_x(1)
            load_x(2)
            load_in(0, 0)
            load_in(0, 1)
            load_x(3)
            load_in(0, 2, slot=2)
            load_in(0, 3, slot=3)
            sp.dma_start(cos_t[:, :], c_cos).then_inc(rope_in, 16)
            sp.dma_start(sin_t[:, :], c_sin).then_inc(rope_in, 16)
            for t in range(4, XTILES):
                load_x(t)
            sp.wait_ge(xn_ready, XTILES)
            sp.dma_start(normw[:, :], norm_ffn_w[0:1, :].broadcast_to([P, D])).then_inc(normw_in, 16)
            iteration(0, True)
            with sp.Fori(1, HEADS) as i:
                iteration(i, False)

            def load_out(m):
                s, _ = raw_slot(H_OUT + m)
                if m >= 2:
                    sp.wait_ge(w_split, H_OUT + m - 3)
                k, nh = KORDER[m // 2], m % 2
                sp.dma_start(raw[:, s, :], w_out_t[:, k, nh * 512:nh * 512 + 512]).then_inc(raw_in[s], 16)

            for m in range(2 * KT):
                load_out(m)
                if m == 9:
                    sp.wait_ge(mix_ready, len(MIX_PARTS) * HEADS)
                    sp.wait_ge(s_new_out, 1 + 16 * HEADS)
                    sp.wait_ge(s_end_out, 1 + 16 * HEADS)
                    sp.dma_start(new_conv_prompt[0, 0].rearrange("w (i p) -> p i w", p=P)[:, :, 0], ncp[:, :, 0], allow_slow_non_contiguous=True).then_inc(conv_out, 16)
                    sp.dma_start(new_conv_prompt[0, 0].rearrange("w (i p) -> p i w", p=P)[:, :, 1], ncp[:, :, 1], allow_slow_non_contiguous=True).then_inc(conv_out, 16)
                    sp.dma_start(new_conv_sample[0, 0].rearrange("w (i p) -> p i w", p=P)[:, :, 0], ncs[:, :, 0], allow_slow_non_contiguous=True).then_inc(conv_out, 16)
                    sp.dma_start(new_conv_sample[0, 0].rearrange("w (i p) -> p i w", p=P)[:, :, 1], ncs[:, :, 1], allow_slow_non_contiguous=True).then_inc(conv_out, 16)
                    sp.dma_start(h[:, 0:2, :], xp_d[0:2 * P, :].rearrange("(t p) n -> p t n", p=P)).then_inc(h_in, 16)
            sp.wait_ge(conv_out, 64)
            sp.dma_start(h[:, 2:8, :], xp_d[2 * P:, :].rearrange("(t p) n -> p t n", p=P)).then_inc(h_rest_in, 16)
            sp.dma_start(h[0:SAMPLE, 8, :], xs_d).then_inc(h_rest_in, 16)

            def load_ffn(g, kind, a, half, n, extra):
                s, _ = raw_slot(n)
                sp.wait_ge(w_split, n - 3 + extra)
                if kind == "wd":
                    src = w_down_t[:, bass.ds(g * FT + a, 1), half * 512:half * 512 + 512].rearrange("p a c -> p (a c)")
                    sp.dma_start(raw[:, s, :], src).then_inc(raw_in[s], 16)
                else:
                    col = (g * FT + a + (FT if kind == "next" else 0)) * P
                    sp.dma_start(raw[:, s, :].rearrange("p (k c) -> p k c", k=4),
                                 w_up_t[:, 4 * half:4 * half + 4, bass.ds(col, P)]).then_inc(raw_in[s], 16)

            def group(g, last):
                for kind, a, half in FFN_ORDER:
                    if not (last and kind == "next"):
                        load_ffn(g, kind, a, half, ffn_half(kind, a, half), g * NF)

            for half in range(2):
                load_ffn(0, "up", 0, half, H_FFN + half, 0)
            with sp.Fori(0, GROUPS - 1) as g:
                group(g, False)
            sp.wait_ge(hw_ready, TILES)
            sp.dma_start(normw[:, :], norm_final_w.rearrange("(a n) -> a n", a=1).broadcast_to([P, D])).then_inc(normw_in, 16)
            group(GROUPS - 1, True)
            for t in range(TILES):
                sp.wait_ge(y_ready, t + 1)
                dst = y_prompt[0, t * P:(t + 1) * P, :] if t < SEQ // P else y_sample[0]
                sp.dma_start(dst, hw[0:rows(t), t % 2, :]).then_inc(y_out[t % 2], 16)
            sp.wait_ge(y_out[0], 16 * ((TILES + 1) // 2))
            sp.wait_ge(y_out[1], 16 * (TILES // 2))

        @block.scalar
        def _(act):
            def split_in(i, n):
                s = n % 2
                act.wait_ge(raw_in[s], 16 * (raw_before(i) + n // 2 + (0 if isinstance(i, int) and i == 0 and n >= 4 else 1)))
                if n >= 2 and s == 0:
                    act.wait_ge(w_used, i * NU + n // 2)
                elif n >= 2:
                    act.wait_ge(proj_done, i * 3 * NU + 3 * (n // 2))
                act.activation(ws_hi[:, s], raw[:, s, :].rearrange("p (k c) -> p k c", k=4), ACT.Copy).then_inc(w_hi, 1)

            def root(t):
                n = xrows(t)
                act.wait_ge(x_in[t % 4], X_COUNT[t])
                if t >= 1:
                    act.wait_ge(ss_ready, t)
                act.activation(junk[0:n, :], xr[0:n, t % 4, :], ACT.Square, accum_out=small[0:n, t % 4, 0:1]).then_inc(ss_ready, 1)
                act.wait_ge(ss_ready, t + 1)
                act.activation(small[0:n, t % 4, 1:2], small[0:n, t % 4, 0:1], ACT.Sqrt, scale=1.0 / D,
                               bias=eps[0:n, :]).then_inc(sd_ready, 1)

            def hi_parts(t):
                n = xrows(t)
                act.wait_ge(xt_done, t + 1)
                for b in range(2):
                    last = act.activation(hn_hi[:, 4 * b:4 * b + 4, t * P:t * P + n],
                                          ps[T_PAIRS[t % 2][b]][:, 0:4 * n].rearrange("p (k c) -> p k c", k=4), ACT.Copy)
                last.then_inc(hn_hi_ready, 1)

            def split_first_k(half):
                act.wait_ge(raw_in[2 + half], 16)
                act.activation(kx_hi[:, half], raw[:, 2 + half, :].rearrange("p (k c) -> p k c", k=4), ACT.Copy).then_inc(w_hi, 1)

            def take_v(i, j, count):
                act.wait_ge(proj_done, count)
                col, n = CGX[j]
                act.activation(vg[:, col:col + n], ps[j][:, 0:n], ACT.Copy).then_inc(proj_act, 1)

            act.wait_ge(eps_ready, 1)
            root(0)
            root(1)
            for t in range(XTILES):
                if t + 2 < XTILES:
                    root(t + 2)
                hi_parts(t)
                if t == 0:
                    split_in(0, 0)
                    split_in(0, 1)
                if t == 2:
                    split_first_k(0)
                    split_first_k(1)
                if t == 5:
                    take_v(0, 0, 1)
            take_v(0, 1, 3)

            def take_unit(i, uname, j):
                act.wait_ge(proj_done, i * 3 * NU + 3 * [x[0] for x in UNITS].index(uname) + j + 1)
                set0 = [x[0] for x in UNITS].index(uname) % 2 * 3
                col, n = dict((x[0], x[2]) for x in UNITS)[uname][j]
                bank = ps[set0 + j]
                if uname == "v":
                    if j == 0:
                        act.wait_ge(proj_dve, NX + i * 12)
                    take_v(i, j, i * 3 * NU + j + 1)
                elif uname == "g":
                    if j == 0:
                        act.wait_ge(ret_done, i * NS + n_step("vC"))
                    act.activation(vg[:, col:col + n], bank[:, 0:n], ACT.Silu).then_inc(proj_act, 1)
                else:
                    if j == 0:
                        act.wait_ge(proj_dve, NX + i * 12)
                    if j < 2:
                        act.activation(u[:, col:col + n], bank[:, 0:n], ACT.Copy).then_inc(proj_act, 1)
                    else:
                        m = META + SEQ - col
                        act.activation(u[:, col:col + m], bank[:, 0:m], ACT.Copy)
                        act.activation(u[:, col + m + 2:TX + 2], bank[:, m:n], ACT.Copy).then_inc(proj_act, 1)

            def take_step(i, name):
                bank = ps[RET[STEPS.index(name) % 2]]
                if name in BY_ACT:
                    act.wait_ge(ret_done, i * NS + n_step(name))
                if name in ("vA", "vB"):
                    c = 0 if name == "vA" else 4
                    act.activation(v_tok[:, c:c + 4, :], bank[:, :].rearrange("p (c e) -> p c e", c=4), ACT.Copy).then_inc(ret_act, 1)
                elif name == "vC":
                    act.activation(v_tok[0:META, 8, :], bank[0:META, 0:HD], ACT.Copy)
                    act.activation(v_tok[0:SAMPLE, 9, :], bank[0:SAMPLE, HD:2 * HD], ACT.Copy).then_inc(ret_act, 1)
                elif name == "kC":
                    act.wait_ge(head_in, 16 * 5 * (i + 1))
                    act.activation(kdC[0:META, 0, :], bank[0:META, 0:HD], ACT.Copy, scale=hc[0:META, C_KMETA:C_KMETA + 1])
                    act.activation(kdC[0:SAMPLE, 1, :], bank[0:SAMPLE, HD:2 * HD], ACT.Copy,
                                   scale=hc[0:SAMPLE, C_KSAMP:C_KSAMP + 1]).then_inc(ret_act, 1)
                elif name in ("kA", "kB"):
                    act.activation(kd[:, :, :], bank[:, :].rearrange("p (c e) -> p c e", c=4), ACT.Copy,
                                   scale=hc[:, C_KDEC:C_KDEC + 1]).then_inc(ret_act, 1)
                elif name in ("oC", "oA", "oB"):
                    w, n = (1, SAMPLE) if name == "oC" else (4, P)
                    act.wait_ge(var_ready, i * 3 + ["oC", "oA", "oB"].index(name) + 1)
                    act.activation(small[0:n, 1, 0:w], small[0:n, 0, 0:w], ACT.Sqrt).then_inc(gsd_ready, 1)
                elif name in ("tC", "tA", "tB"):
                    act.wait_ge(ret_dve, i * len(BY_DVE) + n_dve(name))
                    col, n = {"tC": (SEQ, SAMPLE), "tA": (0, 512), "tB": (512, 512)}[name]
                    src = onC[:, 0:SAMPLE] if name == "tC" else on[:, :, :].rearrange("p c e -> p (c e)")
                    act.activation(mid_hi[:, bass.ds(i + 4, 1), col:col + n].rearrange("p a c -> p (a c)"), src, ACT.Copy).then_inc(mix_hi_ready, 1)

            def tap0(i):
                act.wait_ge(proj_dve, NX + i * 12 + 9)
                act.wait_ge(head_in, 16 * 5 * (i + 1))
                act.activation(u[:, META + SEQ:META + SEQ + 2], hist[:, :], ACT.Copy).then_inc(act_step, 1)
                act.wait_ge(act_step, i + 1)
                for a, w, s in CONV:
                    last = act.activation(y[:, a:a + w], u[:, s:s + w], ACT.Copy, scale=cw[:, 0:1])
                last.then_inc(tap0_ready, 1)

            def conv_hi(i, j):
                act.wait_ge(proj_dve, NX + i * 12 + 9 + j + 1)
                col, n = CGQ[j]
                act.activation(mid_hi[:, bass.ds(i, 1), col - META:col - META + n].rearrange("p a c -> p (a c)"),
                               y[:, col - META:col - META + n], ACT.Copy).then_inc(mix_hi_ready, 1)

            def split_out(m):
                s, before = raw_slot(H_OUT + m)
                act.wait_ge(raw_in[s], 16 * (before + 1))
                act.activation(wo_hi[:, m // 2, m % 2 * 512:m % 2 * 512 + 512], raw[:, s, :], ACT.Copy).then_inc(w_hi, 1)

            def iteration(i, first, last):
                after = AFTER_FIRST if first else AFTER
                for un in range(2 if first else 0, NU):
                    for b in range(6):
                        half = 2 * un + b // 3
                        if b % 3 == 0 and half >= 1 and not (last and half + 1 == HALVES):
                            split_in(i, half + 1)
                        if b >= 3 and UNITS[un][0] in ACT_UNITS:
                            take_unit(i, UNITS[un][0], b - 3)
                        if b >= 3 and UNITS[un][0] == "b":
                            conv_hi(i, b - 3)
                        if (un, b) in after:
                            take_step(i, after[un, b])
                        if (un, b) == (5, 5):
                            tap0(i)
                        if last and un == NU - 1 and b in (3, 4):
                            if b == 3:
                                act.wait_ge(w_used, NU * HEADS)
                            split_out(2 * b - 6)
                            split_out(2 * b - 5)
                if not last:
                    split_in(i, HALVES + 1)

            take_v(0, 2, 5)
            split_in(0, 4)
            iteration(0, True, False)
            with act.Fori(1, HEADS - 1) as i:
                iteration(i, False, False)
            iteration(HEADS - 1, False, True)

            for m in range(4, 2 * KT):
                if m == 8:
                    act.wait_ge(proj_done, 3 * NU * HEADS)
                split_out(m)

            def ht_hi(t):
                n = rows(t)
                act.wait_ge(ht_done, t + 1)
                for b in range(2):
                    last = act.activation(mid_hi[:, 4 * b:4 * b + 4, t * P:t * P + n],
                                          ps[T3(t)[b]][:, 0:4 * n].rearrange("p (k c) -> p k c", k=4), ACT.Copy)
                last.then_inc(ht_hi_ready, 1)

            def split_ffn(g, kind, a, half):
                n = ffn_half(kind, a, half)
                s, before = raw_slot(n)
                act.wait_ge(raw_in[s], 16 * (before + 1) + g * (16 * NF // 4))
                if kind == "wd":
                    act.activation(wd_hi[:, a, half * 512:half * 512 + 512], raw[:, s, :], ACT.Copy).then_inc(w_hi, 1)
                else:
                    act.activation(ws_hi[:, half], raw[:, s, :].rearrange("p (k c) -> p k c", k=4), ACT.Copy).then_inc(w_hi, 1)

            for t in range(TILES):
                ht_hi(t)
                if t == 2:
                    split_ffn(0, "up", 0, 0)
                    split_ffn(0, "up", 0, 1)

            def group(g, last):
                for p in range(8):
                    if 1 <= p:
                        if p % 2 == 1:
                            act.wait_ge(w_used, NU * HEADS + FT * g + p // 2 + 1)
                        else:
                            act.wait_ge(up_done, 12 * g + 3 * (p // 2))
                        split_ffn(g, *FFN_ORDER[2 * p - 2])
                        split_ffn(g, *FFN_ORDER[2 * p - 1])
                    if p % 2 == 1:
                        a = p // 2
                        for j in range(3):
                            n = 3 * a + j
                            w = CGY[j][1]
                            act.wait_ge(up_done, 12 * g + n + 1)
                            act.activation(rl[:, n % 2, 0:w], ps[a % 2 * 3 + j][:, 0:w], ACT.Relu).then_inc(relu_done, 1)
                            act.wait_ge(sq_done, 12 * g + n + 1)
                            act.activation(f_hi[:, a, CGY[j][0]:CGY[j][0] + w], sq[:, n % 2, 0:w], ACT.Copy).then_inc(f_hi_ready, 1)
                if not last:
                    act.wait_ge(up_done, 12 * g + 12)
                    split_ffn(g, "next", 0, 0)
                    split_ffn(g, "next", 0, 1)
                else:
                    for t in range(TILES):
                        act.wait_ge(fin_ms, t + 1)
                        n = rows(t)
                        act.activation(small[0:n, t % 4, 1:2], small[0:n, t % 4, 0:1], ACT.Sqrt).then_inc(fin_sd, 1)

            with act.Fori(0, GROUPS - 1) as g:
                group(g, False)
            group(GROUPS - 1, True)

        @block.vector
        def _(dve):
            chain = {"n": 0, "base": 0}

            def link(ins):
                chain["n"] += 1
                ins.then_inc(dve_step, 1)
                dve.wait_ge(dve_step, chain["n"] + chain["base"])

            def mean_square(src, n, slot, eps=EPS):
                dve.bn_stats(bn[0:n, 0, :], src[:, 0:512])
                link(dve.bn_stats(bn[0:n, 1, :], src[:, 512:1024]))
                link(dve.bn_aggr(mv[0:n, :], bn[0:n, 0:2, :]))
                link(dve.scalar_tensor_tensor(small[0:n, slot, 0:1], mv[0:n, 0:1], mv[0:n, 0:1], mv[0:n, 1:2], ALU.mult, ALU.add))
                return dve.tensor_scalar(small[0:n, slot, 0:1], small[0:n, slot, 0:1], eps, None, ALU.add)

            def split_in(i, n):
                dve.wait_ge(w_hi, i * HALVES + n + 1)
                s = n % 2
                dve.tensor_tensor(ws_lo[:, s], raw[:, s, :].rearrange("p (k c) -> p k c", k=4),
                                  ws_hi[:, s].bitcast(F32), ALU.subtract).then_inc(w_split, 1)

            dve.sem_inc(proj_dve, NX)
            dve.sem_inc(down_taken, 2)
            dve.sem_inc(s_new_out, 1)
            dve.sem_inc(s_end_out, 1)
            dve.memset(eps[:, :], EPS).then_inc(eps_ready, 1)
            dve.wait_ge(const_in, 32)

            def normed(t):
                n = xrows(t)
                dve.wait_ge(sd_ready, t + 1)
                link(dve.reciprocal(small[0:n, t % 4, 2:3], small[0:n, t % 4, 1:2]))
                dve.scalar_tensor_tensor(xr[0:n, t % 4, :], xr[0:n, t % 4, :], small[0:n, t % 4, 2:3], normw[0:n, :],
                                         ALU.mult, ALU.mult).then_inc(xn_ready, 1)

            def lo_parts(t):
                n = xrows(t)
                dve.wait_ge(hn_hi_ready, t + 1)
                for b in range(2):
                    sl = (slice(None), slice(4 * b, 4 * b + 4), slice(t * P, t * P + n))
                    last = dve.tensor_tensor(hn_lo[sl], ps[T_PAIRS[t % 2][b]][:, 0:4 * n].rearrange("p (k c) -> p k c", k=4),
                                             hn_hi[sl].bitcast(F32), ALU.subtract)
                last.then_inc(hn_ready, 1)

            def split_first_k(half):
                dve.wait_ge(w_hi, 3 + half)
                dve.tensor_tensor(kx_lo[:, half], raw[:, 2 + half, :].rearrange("p (k c) -> p k c", k=4),
                                  kx_hi[:, half].bitcast(F32), ALU.subtract).then_inc(w_split, 1)

            link(dve.memset(onC[:, :], 0.0))

            names = [x[0] for x in UNITS]

            def rotary(dst, bank, col, n, at, before):
                dve.tensor_tensor(dst[:, at:at + n], bank[:, 0:n], cos_t[:, col:col + n], ALU.mult)
                dve.wait_ge(proj_dve, before)
                dve.tensor_tensor(rot[0:64, 0:n], bank[64:128, 0:n], sin_t[0:64, col:col + n], ALU.mult)
                link(dve.tensor_tensor(rot[64:128, 0:n], bank[0:64, 0:n], sin_t[64:128, col:col + n], ALU.mult))
                return dve.tensor_tensor(dst[:, at:at + n], dst[:, at:at + n], rot[:, 0:n], ALU.add)

            normed(0)
            for t in range(XTILES):
                if t + 1 < XTILES:
                    normed(t + 1)
                lo_parts(t)
                if t == 0:
                    split_in(0, 0)
                    split_in(0, 1)
                if t == 2:
                    split_first_k(0)
                    split_first_k(1)
                    dve.wait_ge(rope_in, 32)
                if t == 5:
                    dve.wait_ge(proj_done, 2)
                    rotary(kT, ps[3], *CGX[0], CGX[0][0], NX).then_inc(proj_dve, 1)
            dve.wait_ge(proj_done, 4)
            rotary(kT, ps[4], *CGX[1], CGX[1][0], NX + 1).then_inc(proj_dve, 1)
            split_in(0, 4)
            dve.wait_ge(proj_done, 6)
            rotary(kT, ps[5], *CGX[2], CGX[2][0], NX + 2).then_inc(proj_dve, 1)

            def take_unit(i, uname, j):
                un = names.index(uname)
                dve.wait_ge(proj_done, i * 3 * NU + 3 * un + j + 1)
                bank = ps[un % 2 * 3 + j]
                col, n = UNITS[un][2][j]
                if uname == "k":
                    rotary(kT, bank, col, n, col, NX + i * 12 + j).then_inc(proj_dve, 1)
                elif uname == "q":
                    rotary(qT, bank, col, n, col - META, NX + i * 12 + 3 + j).then_inc(proj_dve, 1)
                elif uname == "c":
                    dve.wait_ge(proj_act, i * 9 + 6 + j + 1)
                    m = min(n, META + SEQ - col)
                    ins = dve.tensor_tensor(u[:, col:col + m], bank[:, 0:m], u[:, col:col + m], ALU.mult)
                    if m < n:
                        ins = dve.tensor_tensor(u[:, col + m + 2:TX + 2], bank[:, m:n], u[:, col + m + 2:TX + 2], ALU.mult)
                    ins.then_inc(proj_dve, 1)
                else:
                    a = col - META
                    dve.tensor_tensor(y[:, a:a + n], bank[:, 0:n], y[:, a:a + n], ALU.mult).then_inc(proj_dve, 1)
                    dve.wait_ge(mix_hi_ready, i * 6 + 3 + j + 1)
                    sl = (slice(None), bass.ds(i, 1), slice(a, a + n))
                    dve.tensor_tensor(mid_lo[sl].rearrange("p a c -> p (a c)"), y[:, a:a + n],
                                      mid_hi[sl].rearrange("p a c -> p (a c)").bitcast(F32), ALU.subtract).then_inc(mix_ready, 1)

            def conv(i):
                dve.wait_ge(tap0_ready, i + 1)
                dve.tensor_copy(ncp[:, bass.ds(i, 1), :].rearrange("p a c -> p (a c)"), u[:, META + SEQ - 2:META + SEQ])
                dve.tensor_copy(ncs[:, bass.ds(i, 1), :].rearrange("p a c -> p (a c)"), u[:, TX:TX + 2])
                for tap in (1, 2):
                    for a, w, s in CONV:
                        ins = dve.scalar_tensor_tensor(y[:, a:a + w], u[:, s + tap:s + tap + w], cw[:, tap:tap + 1],
                                                       y[:, a:a + w], ALU.mult, ALU.add)
                    link(ins)

            def take_step(i, name):
                bank = ps[RET[STEPS.index(name) % 2]]
                dve.wait_ge(ret_done, i * NS + n_step(name))
                if name == "UC":
                    dve.wait_ge(head_in, 16 * 5 * (i + 1))
                    dve.wait_ge(s_new_out, 1 + 16 * i)
                    dve.tensor_copy(st[:, 0, :], bank[:, 0:HD])
                    dve.scalar_tensor_tensor(s_new[:, :], s_in[:, :], hc[:, C_G64:C_G64 + 1], bank[:, HD:2 * HD],
                                             ALU.mult, ALU.add).then_inc(ret_dve, 1)
                elif name in ("UA", "UB"):
                    if name == "UA":
                        dve.wait_ge(s_end_out, 1 + 16 * i)
                    c0 = 0 if name == "UA" else 4
                    for c in range(c0, c0 + 4):
                        ins = dve.scalar_tensor_tensor(st[:, (c + 1) % 5, :], st[:, c % 5, :], hc[:, C_G128:C_G128 + 1],
                                                       bank[:, (c - c0) * HD:(c - c0 + 1) * HD], ALU.mult, ALU.add)
                        if c < c0 + 3:
                            link(ins)
                    ins.then_inc(ret_dve, 1)
                elif name == "sC":
                    dve.tensor_tensor(smC[0:SAMPLE, :], bank[0:SAMPLE, 0:SAMPLE], hc[0:SAMPLE, 0:SAMPLE], ALU.mult).then_inc(ret_dve, 1)
                elif name in ("sA", "sB"):
                    mask = hc[:, 0:P].rearrange("p (a j) -> p a j", a=1).broadcast_to([P, 4, P])
                    dve.tensor_tensor(sm[:, :, :], bank[:, :].rearrange("p (c j) -> p c j", c=4), mask, ALU.mult).then_inc(ret_dve, 1)
                elif name in ("oC", "oA", "oB"):
                    w, n = (1, SAMPLE) if name == "oC" else (4, P)
                    for c in range(w):
                        ins = dve.bn_stats(bn[0:n, c, :], bank[0:n, c * HD:(c + 1) * HD])
                    link(ins)
                    m_even, s_even, m_odd, s_odd = (bn[0:n, 0:w, x] for x in (1, 2, 4, 5))
                    mean, diff, tot = (gs[0:n, x, 0:w] for x in range(3))
                    dve.tensor_tensor(mean, m_even, m_odd, ALU.add)
                    dve.tensor_tensor(diff, m_even, m_odd, ALU.subtract)
                    link(dve.tensor_tensor(tot, s_even, s_odd, ALU.add))
                    dve.tensor_scalar(mean, mean, 0.5, None, ALU.mult)
                    link(dve.scalar_tensor_tensor(diff, diff, 0.25, diff, ALU.mult, ALU.mult))
                    link(dve.scalar_tensor_tensor(tot, tot, 1.0 / HD, diff, ALU.mult, ALU.add))
                    ins = dve.tensor_scalar(small[0:n, 0, 0:w], tot, hc[0:n, C_C2:C_C2 + 1], GN_EPS, ALU.mult, ALU.add)
                    ins.then_inc(var_ready, 1)
                    dve.wait_ge(gsd_ready, i * 3 + ["oC", "oA", "oB"].index(name) + 1)
                    link(dve.reciprocal(small[0:n, 2, 0:w], small[0:n, 1, 0:w]))
                    link(dve.tensor_scalar(small[0:n, 3, 0:w], small[0:n, 2, 0:w], hc[0:n, C_C:C_C + 1], None, ALU.mult))
                    for c in range(w):
                        dst = onC[0:n, :] if name == "oC" else on[:, c, :]
                        ins = dve.tensor_scalar(dst, bank[0:n, c * HD:(c + 1) * HD], gs[0:n, 0, c:c + 1], small[0:n, 3, c:c + 1],
                                                ALU.subtract, ALU.mult)
                    ins.then_inc(ret_dve, 1)
                elif name in ("tC", "tA", "tB"):
                    dve.wait_ge(proj_act, i * 9 + 6)
                    col, n = {"tC": (SEQ, SAMPLE), "tA": (0, 512), "tB": (512, 512)}[name]
                    og = onC[:, 0:SAMPLE] if name == "tC" else on[:, :, :].rearrange("p c e -> p (c e)")
                    dve.scalar_tensor_tensor(og, bank[:, 0:n], gnw[:, 0:1], vg[:, META + col:META + col + n],
                                             ALU.mult, ALU.mult).then_inc(ret_dve, 1)
                    dve.wait_ge(mix_hi_ready, i * 6 + MIX_PARTS.index(name) + 1)
                    sl = (slice(None), bass.ds(i + 4, 1), slice(col, col + n))
                    dve.tensor_tensor(mid_lo[sl].rearrange("p a c -> p (a c)"), og,
                                      mid_hi[sl].rearrange("p a c -> p (a c)").bitcast(F32), ALU.subtract).then_inc(mix_ready, 1)

            def split_out(m):
                dve.wait_ge(w_hi, H_OUT + m + 1)
                s, _ = raw_slot(H_OUT + m)
                sl = (slice(None), m // 2, slice(m % 2 * 512, m % 2 * 512 + 512))
                dve.tensor_tensor(wo_lo[sl], raw[:, s, :], wo_hi[sl].bitcast(F32), ALU.subtract).then_inc(w_split, 1)

            def iteration(i, first, last):
                after = AFTER_FIRST if first else AFTER
                for un in range(2 if first else 0, NU):
                    for b in range(6):
                        half = 2 * un + b // 3
                        if b % 3 == 0 and half >= 1 and not (last and half + 1 == HALVES):
                            split_in(i, half + 1)
                        if (un, b) == (NU - 1, 0):
                            conv(i)
                        if b >= 3 and names[un] in DVE_UNITS:
                            take_unit(i, names[un], b - 3)
                        if (un, b) in after and after[un, b] in BY_DVE:
                            take_step(i, after[un, b])
                        if last and un == NU - 1 and b in (3, 4):
                            split_out(2 * b - 6)
                            split_out(2 * b - 5)
                if not last:
                    split_in(i, HALVES + 1)

            LINKS = 32
            iteration(0, True, False)
            start = chain["n"]
            with dve.Fori(1, HEADS - 1) as i:
                chain["base"] = (i - 1) * LINKS
                iteration(i, False, False)
            assert chain["n"] == start + LINKS, chain["n"] - start
            chain.update(n=start + (HEADS - 2) * LINKS, base=0)
            iteration(HEADS - 1, False, True)

            for m in range(4, 2 * KT):
                split_out(m)
            dve.wait_ge(normw_in, 16)

            def residual(t):
                n = rows(t)
                dve.wait_ge(out_done, t + 1)
                if t == 0:
                    dve.wait_ge(h_in, 16)
                if t == 2:
                    dve.wait_ge(h_rest_in, 32)
                pair = PAIRS3[t if t < 2 else (2 * t - 1) % 4]
                for nh in range(2):
                    sl = slice(nh * 512, nh * 512 + 512)
                    ins = dve.tensor_tensor(h[0:n, t, sl], ps[pair[nh]][0:n, :], h[0:n, t, sl], ALU.add)
                ins.then_inc(out_taken, 1)
                dve.wait_ge(out_taken, t + 1)
                if t >= 2:
                    dve.wait_ge(ht_done, t - 1)
                dve.tensor_tensor(hw[0:n, t % 2, :], h[0:n, t, :], normw[0:n, :], ALU.mult).then_inc(hw_ready, 1)

            def inverse_ms(t):
                n = rows(t)
                link(mean_square(h[0:n, t, :], n, 0))
                dve.reciprocal(inv_ms[0:n, t:t + 1], small[0:n, 0, 0:1]).then_inc(ms2_ready, 1)

            def ht_lo(t):
                n = rows(t)
                dve.wait_ge(ht_hi_ready, t + 1)
                for b in range(2):
                    sl = (slice(None), slice(4 * b, 4 * b + 4), slice(t * P, t * P + n))
                    last = dve.tensor_tensor(mid_lo[sl], ps[T3(t)[b]][:, 0:4 * n].rearrange("p (k c) -> p k c", k=4),
                                             mid_hi[sl].bitcast(F32), ALU.subtract)
                last.then_inc(ht_ready, 1)

            def split_ffn(g, kind, a, half):
                n = ffn_half(kind, a, half)
                s, _ = raw_slot(n)
                dve.wait_ge(w_hi, n + 1 + g * NF)
                if kind == "wd":
                    sl = (slice(None), a, slice(half * 512, half * 512 + 512))
                    dve.tensor_tensor(wd_lo[sl], raw[:, s, :], wd_hi[sl].bitcast(F32), ALU.subtract).then_inc(w_split, 1)
                else:
                    dve.tensor_tensor(ws_lo[:, half], raw[:, s, :].rearrange("p (k c) -> p k c", k=4),
                                      ws_hi[:, half].bitcast(F32), ALU.subtract).then_inc(w_split, 1)

            residual(0)
            residual(1)
            inverse_ms(0)
            inverse_ms(1)
            ht_lo(0)
            for t in range(2, TILES):
                residual(t)
                ht_lo(t - 1)
                if t == 3:
                    split_ffn(0, "up", 0, 0)
                    split_ffn(0, "up", 0, 1)
                if t < TILES - 1:
                    inverse_ms(t)
            ht_lo(TILES - 1)
            inverse_ms(TILES - 1)

            def take_down(g, t):
                n = rows(t)
                dve.wait_ge(down_done, 9 * g + t + 1)
                pair = DOWN_PAIRS[t % 3]
                for nh in range(2):
                    sl = slice(nh * 512, nh * 512 + 512)
                    ins = dve.scalar_tensor_tensor(h[0:n, t, sl], ps[pair[nh]][0:n, :], inv_ms[0:n, t:t + 1], h[0:n, t, sl],
                                                   ALU.mult, ALU.add)
                ins.then_inc(down_taken, 1)

            def group(g, last):
                for p in range(8):
                    if 1 <= p:
                        split_ffn(g, *FFN_ORDER[2 * p - 2])
                        split_ffn(g, *FFN_ORDER[2 * p - 1])
                    if p % 2 == 1:
                        a = p // 2
                        for j in range(3):
                            n = 3 * a + j
                            w = CGY[j][1]
                            sl = (slice(None), a, slice(CGY[j][0], CGY[j][0] + w))
                            dve.wait_ge(relu_done, 12 * g + n + 1)
                            dve.tensor_tensor(sq[:, n % 2, 0:w], rl[:, n % 2, 0:w], rl[:, n % 2, 0:w], ALU.mult).then_inc(sq_done, 1)
                            dve.wait_ge(f_hi_ready, 12 * g + n + 1)
                            dve.tensor_tensor(f_lo[sl], sq[:, n % 2, 0:w], f_hi[sl].bitcast(F32), ALU.subtract).then_inc(f_ready, 1)
                if not last:
                    split_ffn(g, "next", 0, 0)
                    split_ffn(g, "next", 0, 1)
                for t in range(TILES):
                    take_down(g, t)
                    if last:
                        n = rows(t)
                        dve.wait_ge(down_taken, 2 + 9 * g + t + 1)
                        mean_square(h[0:n, t, :], n, t % 4).then_inc(fin_ms, 1)
                        dve.wait_ge(fin_sd, t + 1)
                        link(dve.reciprocal(small[0:n, t % 4, 2:3], small[0:n, t % 4, 1:2]))
                        if t >= 2:
                            dve.wait_ge(y_out[t % 2], 16 * (t // 2))
                        dve.scalar_tensor_tensor(hw[0:n, t % 2, :], h[0:n, t, :], small[0:n, t % 4, 2:3], normw[0:n, :],
                                                 ALU.mult, ALU.mult).then_inc(y_ready, 1)

            with dve.Fori(0, GROUPS - 1) as g:
                group(g, False)
            dve.wait_ge(normw_in, 32)
            group(GROUPS - 1, True)

        @block.tensor
        def _(pe):
            def passes(out, a_hi, a_lo, b_hi, b_lo, start, stop):
                pe.matmul(out, a_hi, b_hi, start=start, stop=False)
                pe.matmul(out, a_hi, b_lo, start=False, stop=False)
                return pe.matmul(out, a_lo, b_hi, start=False, stop=stop)

            def transposed_x(t):
                n = xrows(t)
                pe.wait_ge(xn_ready, t + 1)
                if t >= 2:
                    pe.wait_ge(hn_ready, t - 1)
                for k in range(KT):
                    last = pe.transpose(ps[T_PAIRS[t % 2][k // 4]][:, k % 4 * n:k % 4 * n + n],
                                        xr[0:n, t % 4, k * P:(k + 1) * P], ident[0:n, 0:n])
                last.then_inc(xt_done, 1)

            pe.wait_ge(const_in, 32)
            for t in range(3):
                transposed_x(t)
            for j, (col, w) in enumerate(CGX):
                pe.wait_ge(hn_ready, 3 * (j + 1))
                for un, (a_hi, a_lo) in enumerate(((ws_hi, ws_lo), (kx_hi, kx_lo))):
                    for half in range(2):
                        pe.wait_ge(w_split, 2 * un + half + 1)
                        for k in range(4):
                            kk = 4 * half + k
                            last = passes(ps[3 * un + j][:, 0:w], a_hi[:, half, k, :], a_lo[:, half, k, :],
                                          hn_hi[:, kk, col:col + w], hn_lo[:, kk, col:col + w],
                                          start=kk == 0, stop=kk == KT - 1)
                        if half == 1:
                            last.then_inc(proj_done, 1)
                        elif j == 2:
                            last.then_inc(w_used, 1)
                        if j < 2 and 2 * un + half < 3:
                            transposed_x(3 * (j + 1) + 2 * un + half)

            names = [x[0] for x in UNITS]

            def bank_free(i, un, j):
                name = names[un]
                if name == "v":
                    pe.wait_ge(proj_dve, i * 12 + j + 1)
                elif name == "q":
                    pe.wait_ge(proj_act, i * 9 + j + 1)
                elif name == "g":
                    pe.wait_ge(proj_dve, NX + i * 12 + j + 1)
                elif name == "xt":
                    pe.wait_ge(proj_dve, NX + i * 12 + 3 + j + 1)
                elif name == "c":
                    pe.wait_ge(proj_act, i * 9 + 3 + j + 1)
                elif name == "b":
                    pe.wait_ge(proj_act, i * 9 + 6 + j + 1)

            def step(i, name):
                s = STEPS.index(name)
                out = ps[RET[s % 2]]
                if s < 2:
                    pe.wait_ge(proj_dve, NX + i * 12)
                elif STEPS[s - 2] in BY_ACT:
                    pe.wait_ge(ret_act, i * len(BY_ACT) + n_act(STEPS[s - 2]))
                else:
                    pe.wait_ge(ret_dve, i * len(BY_DVE) + n_dve(STEPS[s - 2]))
                c0 = 4 if name[1] == "B" else 0
                if name[0] in "vk" and name[1] in "AB":
                    src = vg if name[0] == "v" else kT
                    if name[0] == "v":
                        pe.wait_ge(proj_act, i * 9 + (2 if name == "vA" else 3))
                    for c in range(4):
                        at = META + (c0 + c) * P
                        last = pe.transpose(out[:, c * P:(c + 1) * P], src[:, at:at + P], ident[:, :])
                elif name in ("vC", "kC"):
                    src = vg if name == "vC" else kT
                    if name == "kC":
                        pe.wait_ge(proj_dve, NX + i * 12 + 3)
                    pe.transpose(out[0:META, 0:HD], src[:, 0:META], ident[:, :])
                    last = pe.transpose(out[0:SAMPLE, HD:2 * HD], src[:, META + SEQ:TX], ident[:, :])
                elif name == "UC":
                    pe.wait_ge(ret_act, i * len(BY_ACT) + n_act("kC"))
                    pe.matmul(out[:, 0:HD], kdC[0:META, 0, :], v_tok[0:META, 8, :], start=True, stop=True)
                    last = pe.matmul(out[:, HD:2 * HD], kdC[0:SAMPLE, 1, :], v_tok[0:SAMPLE, 9, :], start=True, stop=True)
                elif name in ("UA", "UB"):
                    pe.wait_ge(ret_act, i * len(BY_ACT) + n_act("kA" if name == "UA" else "kB"))
                    for c in range(4):
                        last = pe.matmul(out[:, c * HD:(c + 1) * HD], kd[:, c, :], v_tok[:, c0 + c, :], start=True, stop=True)
                elif name == "sC":
                    pe.wait_ge(proj_dve, NX + i * 12 + 6)
                    last = pe.matmul(out[0:SAMPLE, 0:SAMPLE], kT[:, META + SEQ:TX], qT[:, SEQ:TY], start=True, stop=True)
                elif name in ("sA", "sB"):
                    for c in range(4):
                        at = (c0 + c) * P
                        last = pe.matmul(out[:, c * P:(c + 1) * P], kT[:, META + at:META + at + P], qT[:, at:at + P], start=True, stop=True)
                elif name == "oC":
                    pe.wait_ge(ret_dve, i * len(BY_DVE) + n_dve("sC"))
                    pe.wait_ge(head_in, 16 * 5 * (i + 1))
                    pe.matmul(out[0:SAMPLE, 0:HD], qT[:, SEQ:TY], s_in[:, :], start=True, stop=False)
                    last = pe.matmul(out[0:SAMPLE, 0:HD], smC[0:SAMPLE, :], v_tok[0:SAMPLE, 9, :], start=False, stop=True)
                elif name in ("oA", "oB"):
                    pe.wait_ge(ret_dve, i * len(BY_DVE) + n_dve("sA" if name == "oA" else "sB"))
                    for c in range(4):
                        at = (c0 + c) * P
                        pe.matmul(out[:, c * HD:(c + 1) * HD], sm[:, c, :], v_tok[:, c0 + c, :], start=True, stop=False)
                        last = pe.matmul(out[:, c * HD:(c + 1) * HD], qT[:, at:at + P], st[:, (c0 + c) % 5, :], start=False, stop=True)
                elif name == "tC":
                    last = pe.transpose(out[:, 0:P], onC[:, :], ident[:, :])
                else:
                    pe.wait_ge(ret_dve, i * len(BY_DVE) + n_dve("oA" if name == "tA" else "oB"))
                    for c in range(4):
                        last = pe.transpose(out[:, c * P:(c + 1) * P], on[:, c, :], ident[:, :])
                last.then_inc(ret_done, 1)

            def iteration(i, first):
                after = AFTER_FIRST if first else AFTER
                for un in range(2 if first else 0, NU):
                    groups = UNITS[un][2]
                    for half in range(2):
                        n = 2 * un + half
                        pe.wait_ge(w_split, i * HALVES + n + 1)
                        for j, (col, w) in enumerate(groups):
                            if half == 0:
                                bank_free(i, un, j)
                            out = ps[un % 2 * 3 + j][:, 0:w]
                            for k in range(4):
                                kk = 4 * half + k
                                last = passes(out, ws_hi[:, n % 2, k, :], ws_lo[:, n % 2, k, :],
                                              hn_hi[:, kk, col:col + w], hn_lo[:, kk, col:col + w],
                                              start=kk == 0, stop=kk == KT - 1)
                            if half == 1:
                                last.then_inc(proj_done, 1)
                            if (un, 3 * half + j) in after and j < 2:
                                step(i, after[un, 3 * half + j])
                        if half == 0:
                            last.then_inc(w_used, 1)
                        if (un, 3 * half + 2) in after:
                            step(i, after[un, 3 * half + 2])

            iteration(0, True)
            with pe.Fori(1, HEADS) as i:
                iteration(i, False)

            def out_pair(t):
                return PAIRS3[t if t < 2 else (2 * t - 1) % 4]

            def out_part(t, i, k):
                n = rows(t)
                for nh in range(2):
                    sl = slice(nh * 512, nh * 512 + 512)
                    last = passes(ps[out_pair(t)[nh]][0:n, :], mid_hi[:, k, t * P:t * P + n], mid_lo[:, k, t * P:t * P + n],
                                  wo_hi[:, i, sl], wo_lo[:, i, sl], start=i == 0, stop=i == KT - 1)
                return last

            def transposed(t):
                n = rows(t)
                pe.wait_ge(hw_ready, t + 1)
                if t == 1:
                    pe.wait_ge(out_taken, 1)
                elif t == TILES - 1:
                    pe.wait_ge(out_taken, TILES - 1)
                elif t >= 2:
                    pe.wait_ge(ht_ready, t - 1)
                for k in range(KT):
                    last = pe.transpose(ps[T3(t)[k // 4]][:, k % 4 * n:k % 4 * n + n],
                                        hw[0:n, t % 2, k * P:(k + 1) * P], ident[0:n, 0:n])
                last.then_inc(ht_done, 1)

            pe.wait_ge(ret_dve, len(BY_DVE) * HEADS)
            for i, k in enumerate(KORDER):
                pe.wait_ge(w_split, H_OUT + 2 * i + 2)
                pe.wait_ge(mix_ready, len(MIX_PARTS) * HEADS - (3 if k >= 4 else 0))
                for t in range(2):
                    last = out_part(t, i, k)
                    if i == KT - 1:
                        last.then_inc(out_done, 1)
            for t in range(2, TILES):
                if t == 2:
                    pe.wait_ge(proj_dve, NX + 12 * HEADS)
                else:
                    pe.wait_ge(out_taken, t - 1)
                for i, k in enumerate(KORDER):
                    last = out_part(t, i, k)
                last.then_inc(out_done, 1)
                transposed(t - 2)
            transposed(TILES - 2)

            def group(g, first):
                for a in range(FT):
                    for half in range(2):
                        slot = half
                        if a == 0:
                            pe.wait_ge(w_split, H_FFN + half + 1 + g * NF)
                        else:
                            pe.wait_ge(w_split, ffn_half("up", a, half) + 1 + g * NF)
                        for j, (col, w) in enumerate(CGY):
                            if half == 0:
                                if first and a == 0:
                                    if j == 2:
                                        transposed(TILES - 1)
                                    pe.wait_ge(ht_ready, [7, 7, 9][j])
                                elif a == 0:
                                    pe.wait_ge(down_taken, 9 * g + (0 if j < 2 else 1))
                                elif a == 1:
                                    if not first:
                                        pe.wait_ge(relu_done, 12 * g)
                                        pe.wait_ge(down_taken, 9 * g + 1)
                                else:
                                    pe.wait_ge(relu_done, 12 * g + 3 * (a - 2) + j + 1)
                            out = ps[a % 2 * 3 + j][:, 0:w]
                            for k in range(4):
                                kk = 4 * half + k
                                last = passes(out, ws_hi[:, slot, k, :], ws_lo[:, slot, k, :],
                                              mid_hi[:, kk, col:col + w], mid_lo[:, kk, col:col + w],
                                              start=kk == 0, stop=kk == KT - 1)
                            if half == 1:
                                last.then_inc(up_done, 1)
                        if half == 0:
                            last.then_inc(w_used, 1)
                for t in range(TILES):
                    n = rows(t)
                    if t == 0:
                        pe.wait_ge(w_split, ffn_half("wd", 3, 1) + 1 + g * NF)
                    pe.wait_ge(f_ready, 12 * g + 9 + 1 + (t * P + n - 1) // BLK)
                    if t == 1:
                        pe.wait_ge(relu_done, 12 * g + 10)
                    elif t == 2:
                        pe.wait_ge(down_taken, 2 + 9 * g)
                    elif t >= 3:
                        pe.wait_ge(down_taken, 2 + 9 * g + t - 2)
                    for nh in range(2):
                        sl = slice(nh * 512, nh * 512 + 512)
                        for a in range(FT):
                            last = passes(ps[DOWN_PAIRS[t % 3][nh]][0:n, :], f_hi[:, a, t * P:t * P + n],
                                          f_lo[:, a, t * P:t * P + n], wd_hi[:, a, sl], wd_lo[:, a, sl],
                                          start=a == 0, stop=a == FT - 1)
                    last.then_inc(down_done, 1)

            group(0, True)
            with pe.Fori(1, GROUPS) as g:
                group(g, False)


_INS = ["x_prompt", "x_sample", "state_conv", "state_ret", "meta_tokens", "norm_mix_w", "w_in", "conv_w", "ret_gn_w",
        "w_out", "norm_ffn_w", "w_up", "w_down", "norm_final_w"]
_OUTS = [(1, SEQ, D), (1, SAMPLE, D), (1, 1, 2, DC), (1, 1, HEADS, HD, HD), (1, 1, 2, DC), (1, 1, HEADS, HD, HD)]


def kernel(**inputs):
    import concourse.bacc as bacc
    from concourse.bass_utils import run_bass_kernel_spmd

    nc = bacc.Bacc("TRN2", target_bir_lowering=False, num_devices=1)
    arrays, args = {}, []
    for name, a in [(n, np.ascontiguousarray(inputs[n])) for n in _INS] + list(constants().items()):
        arrays[f"in_{name}"] = a
        args.append(nc.dram_tensor(f"in_{name}", a.shape, mybir.dt.from_np(a.dtype), kind="ExternalInput").ap())
    for i, shape in enumerate(_OUTS):
        args.append(nc.dram_tensor(f"out_{i}", shape, F32, kind="ExternalOutput").ap())
    build(nc, *args)
    r = run_bass_kernel_spmd(nc, [arrays], core_ids=[0])
    return tuple(r.results[0][f"out_{i}"] for i in range(len(_OUTS)))
```

```python
from contextlib import ExitStack

import numpy as np

import concourse.bass as bass
from concourse import mybir

F32 = mybir.dt.float32
F32R = mybir.dt.float32r
ALU = mybir.AluOpType
ACT = mybir.ActivationFunctionType

P = 128
D = 1024
SEQ = 1024
SAMPLE = 64
PAST = 256
META = 16
DC = 512
HEADS = 4
HD = 128
FF = 4 * D
DIN = 3 * DC + 4 * HEADS * HD
EPS = 1e-6
GN_EPS = 1e-5

KT = D // P
TX = META + SEQ + SAMPLE
TY = SEQ + SAMPLE
TP = TY + SAMPLE
TILES = (TY + P - 1) // P
XTILES = (TX + P - 1) // P
BLK = 368
CGX = [(0, 368), (368, 368), (736, 368)]
CGQ = [(16, 352), (368, 368), (736, 368)]
CGY = [(0, 368), (368, 368), (736, 352)]

CONV = [(0, SEQ, META - 2), (SEQ, SAMPLE, META + SEQ)]
UNITS = [("v", 3 * DC + 2 * DC, CGX), ("k", 3 * DC + DC, CGX), ("q", 3 * DC, CGQ),
         ("g", 3 * DC + 3 * DC, CGQ), ("xt", 0, CGX), ("c", 2 * DC, CGX), ("b", DC, CGQ)]
NU = len(UNITS)
HALVES = 2 * NU
STEPS = ["vA", "vB", "vC", "kC", "UC", "kA", "UA", "sC", "sA", "oC", "oA", "kB", "UB", "tC", "tA",
         "sB", "oB", "tB"]
FIRST = {"vA": (2, 0), "vB": (2, 1), "vC": (2, 2), "kC": (2, 3), "UC": (2, 4), "kA": (2, 5), "UA": (3, 0)}
AFTER = {(1, 1): "vA", (1, 2): "vB", (1, 3): "vC", (2, 2): "kC", (2, 3): "UC", (2, 4): "kA",
         (2, 5): "UA", (3, 2): "sC", (3, 3): "sA", (3, 4): "oC", (3, 5): "oA", (4, 0): "kB",
         (4, 1): "UB", (4, 2): "tC", (4, 3): "tA", (4, 4): "sB", (5, 1): "oB", (5, 5): "tB"}
NS = len(STEPS)
AFTER_FIRST = {**{at: s for at, s in AFTER.items() if s not in FIRST}, **{at: s for s, at in FIRST.items()}}
BY_ACT = ["vA", "vB", "vC", "kC", "kA", "kB"]
BY_DVE = [s for s in STEPS if s not in BY_ACT]
ACT_UNITS = ["v", "g", "xt"]
DVE_UNITS = ["k", "q", "c", "b"]
MIX_PARTS = ["tC", "tA", "tB", 0, 1, 2]
KORDER = [4, 5, 6, 7, 0, 1, 2, 3]
GROUPS = 8
FT = FF // GROUPS // P
C_MASK, C_KDEC, C_KMETA, C_KSAMP, C_C, C_C2, C_G128, C_G64, NCONST = 0, 128, 129, 130, 131, 132, 133, 134, 135


def constants():
    half = HD // 2
    inv = (np.float32(10000.0) ** (-np.arange(half, dtype=np.float32) / np.float32(half))).astype(np.float32)
    pos = np.concatenate([np.arange(META + SEQ) - META, np.arange(SAMPLE) + PAST]).astype(np.float32)
    ang = (pos[None, :] * inv[:, None]).astype(np.float32).astype(np.float64)
    cos = np.concatenate([np.cos(ang), np.cos(ang)]).astype(np.float32)
    sin = np.concatenate([-np.sin(ang), np.sin(ang)]).astype(np.float32)
    head = np.zeros((HEADS, P, NCONST), np.float64)
    j = np.arange(P)
    scale = HD ** -0.5
    for h in range(HEADS):
        lg = np.log(1.0 - 2.0 ** (-5.0 - h))
        head[h, :, :P] = np.where(j[None, :] >= j[:, None], np.exp(-(j[:, None] + 1) * lg), 0.0) * scale
        head[h, :, C_KDEC] = np.exp((P - 1 - j) * lg) * scale
        head[h, :META, C_KMETA] = np.exp((META - 1 - j[:META]) * lg) * scale
        head[h, :SAMPLE, C_KSAMP] = np.exp((SAMPLE - 1 - j[:SAMPLE]) * lg) * scale
        head[h, :, C_C] = np.exp((j + 1) * lg)
        head[h, :, C_C2] = np.exp(2 * (j + 1) * lg)
        head[h, :, C_G128] = np.exp(P * lg)
        head[h, :, C_G64] = np.exp(SAMPLE * lg)
    return {"c_cos": cos, "c_sin": sin, "c_head": head.astype(np.float32), "c_ident": np.eye(P, dtype=np.float32)}


def build(nc, x_prompt, x_sample, state_conv, state_ret, meta_tokens, norm_mix_w, w_in, conv_w, ret_gn_w,
          w_out, norm_ffn_w, w_up, w_down, norm_final_w, c_cos, c_sin, c_head, c_ident,
          y_prompt, y_sample, new_conv_prompt, new_ret_prompt, new_conv_sample, new_ret_sample):
    ctx = ExitStack()
    with ctx:
        base = (nc.sbuf_base + 31) // 32 * 32
        place = {"at": base}

        def region(size):
            at = place["at"]
            place["at"] = at + (size + 31) // 32 * 32
            return at

        def sb(name, shape, at, dt=F32):
            return nc.alloc_sbuf_tensor_at(name, shape, dt, offset=at)

        r1 = region(2 * KT * TX * 4)
        hn_hi = sb("hn_hi", [P, KT, TX], r1, F32R)
        hn_lo = sb("hn_lo", [P, KT, TX], r1 + KT * TX * 4, F32R)
        wo_hi = sb("wo_hi", [P, KT, D], r1, F32R)
        wo_lo = sb("wo_lo", [P, KT, D], r1 + KT * TX * 4, F32R)
        f_hi = sb("f_hi", [P, FT, TP], r1, F32R)
        f_lo = sb("f_lo", [P, FT, SEQ], r1 + FT * TP * 4, F32R)
        wd_hi = sb("wd_hi", [P, FT, D], r1 + FT * (TP + SEQ) * 4, F32R)
        wd_lo = sb("wd_lo", [P, FT, D], r1 + FT * (TP + SEQ + D) * 4, F32R)
        sq = sb("sq", [P, 2, BLK], r1 + FT * (TP + SEQ + 2 * D) * 4)
        assert FT * (TP + SEQ + 2 * D) + 2 * BLK <= 2 * KT * TX
        r2 = region(KT * (TP + TY) * 4)
        xr = sb("xr", [P, 4, D], r2)
        mid_hi = sb("mid_hi", [P, KT, TP], r2, F32R)
        mid_lo = sb("mid_lo", [P, KT, TY], r2 + KT * TP * 4, F32R)
        ws_hi = sb("ws_hi", [P, 2, 4, P], region(4096), F32R)
        ws_lo = sb("ws_lo", [P, 2, 4, P], region(4096), F32R)
        raw = sb("raw", [P, 4, 512], region(8192))
        r_norm = region(4096)
        normw = sb("normw", [P, D], r_norm)
        kd = sb("kd", [P, 4, HD], r_norm)
        kdC = sb("kdC", [P, 2, HD], r_norm + 2048)
        s_in = sb("s_in", [P, HD], r_norm + 3072)
        s_new = sb("s_new", [P, HD], r_norm + 3584)
        ident = sb("ident", [P, P], region(512))
        bn = sb("bn", [P, 4, 6], region(96))
        mv = sb("mv", [P, 2], region(8))
        gs = sb("gs", [P, 3, 4], region(48))
        small = sb("small", [P, 4, 4], region(64))
        inv_ms = sb("inv_ms", [P, TILES], region(36))
        eps = sb("eps", [P, 1], region(4))
        r3 = place["at"]

        v_tok = sb("v_tok", [P, 10, HD], region(10 * HD * 4))
        u = sb("u", [P, TX + 2], region((TX + 2) * 4))
        y = sb("y", [P, TY], region(TY * 4))
        cos_t = sb("cos_t", [P, TX], region(TX * 4))
        sin_t = sb("sin_t", [P, TX], region(TX * 4))
        qT = sb("qT", [P, TY], region(TY * 4))
        kT = sb("kT", [P, TX], region(TX * 4))
        vg = sb("vg", [P, TX], region(TX * 4))
        sm = sb("sm", [P, 4, P], region(2048))
        on = sb("on", [P, 4, HD], region(2048))
        st = sb("st", [P, 5, HD], region(2560))
        smC = sb("smC", [P, SAMPLE], region(256))
        onC = sb("onC", [P, HD], region(512))
        rot = sb("rot", [P, BLK], region(BLK * 4))
        hc = sb("hc", [P, NCONST], region(NCONST * 4))
        gnw = sb("gnw", [P, 1], region(4))
        cw = sb("cw", [P, 3], region(12))
        hist = sb("hist", [P, 2], region(8))
        ncp = sb("ncp", [P, HEADS, 2], region(32))
        ncs = sb("ncs", [P, HEADS, 2], region(32))
        end2 = place["at"]

        place["at"] = r3
        kx_hi = sb("kx_hi", [P, 2, 4, P], region(4096), F32R)
        kx_lo = sb("kx_lo", [P, 2, 4, P], region(4096), F32R)
        junk = sb("junk", [P, D], region(4096))

        place["at"] = r3
        h = sb("h", [P, TILES, D], region(TILES * D * 4))
        hw = sb("hw", [P, 2, D], region(2 * D * 4))
        rl = sb("rl", [P, 2, BLK], region(2 * BLK * 4))
        assert max(end2, place["at"]) <= nc.sbuf_usable_end, (end2, place["at"], nc.sbuf_usable_end)

        ps = [ctx.enter_context(nc.psum_tensor(f"ps{n}", [P, 512], F32)) for n in range(8)]
        def T1(t):
            return (1, 4) if t == 2 else [(2, 5), (6, 7)][t % 2]

        RET = [6, 7]
        OUT_PAIRS = [(4, 5), (6, 7)]
        def T3(t):
            return [(0, 1), (2, 3)][t % 2] if t < TILES - 1 else (6, 7)

        DOWN_ORDER = [*range(TILES - 2), TILES - 1, TILES - 2]
        DOWN_PAIRS = [(0, 1), (2, 3), (6, 7)]

        def sem(name):
            return ctx.enter_context(nc.semaphore(name))

        eps_ready = sem("eps_ready")
        warm_ready = sem("warm_ready")
        act_step = sem("act_step")
        const_in = sem("const_in")
        rope_in = sem("rope_in")
        x_in = [sem(f"x_in{n}") for n in range(4)]
        ss_ready = sem("ss_ready")
        sd_ready = sem("sd_ready")
        xn_ready = sem("xn_ready")
        xt_done = sem("xt_done")
        hn_hi_ready = sem("hn_hi_ready")
        hn_ready = sem("hn_ready")
        raw_in = [sem(f"raw_in{n}") for n in range(4)]
        w_hi = sem("w_hi")
        w_split = sem("w_split")
        w_used = sem("w_used")
        proj_done = sem("proj_done")
        proj_act = sem("proj_act")
        proj_dve = sem("proj_dve")
        ret_done = sem("ret_done")
        ret_act = sem("ret_act")
        ret_dve = sem("ret_dve")
        head_in = sem("head_in")
        var_ready = sem("var_ready")
        gsd_ready = sem("gsd_ready")
        mix_hi_ready = sem("mix_hi_ready")
        mix_ready = sem("mix_ready")
        s_new_out = sem("s_new_out")
        s_end_out = sem("s_end_out")
        conv_out = sem("conv_out")
        normw_in = sem("normw_in")
        h_in = sem("h_in")
        h_rest_in = sem("h_rest_in")
        out_done = sem("out_done")
        out_taken = sem("out_taken")
        hw_ready = sem("hw_ready")
        ht_done = sem("ht_done")
        ht_hi_ready = sem("ht_hi_ready")
        ht_ready = sem("ht_ready")
        ms2_ready = sem("ms2_ready")
        tap0_ready = sem("tap0_ready")
        up_done = sem("up_done")
        relu_done = sem("relu_done")
        sq_done = sem("sq_done")
        f_hi_ready = sem("f_hi_ready")
        f_ready = sem("f_ready")
        down_done = sem("down_done")
        down_taken = sem("down_taken")
        fin_half = sem("fin_half")
        fin_step = sem("fin_step")
        fin_sd = sem("fin_sd")
        y_ready = sem("y_ready")
        y_out = [sem("y_out0"), sem("y_out1")]
        dve_step = sem("dve_step")
        NX = 3

        w_in_t = w_in[0].rearrange("(k p) n -> p k n", p=P)
        w_up_t = w_up[0].rearrange("(k p) n -> p k n", p=P)
        w_out_t = w_out[0].rearrange("(k p) n -> p k n", p=P)
        w_down_t = w_down[0].rearrange("(k p) n -> p k n", p=P)
        meta_d, xp_d, xs_d = meta_tokens, x_prompt[0], x_sample[0]

        def x_rows(t):
            lo, hi = t * P, min((t + 1) * P, TX)
            out = []
            for src, a, b in ((meta_d, 0, META), (xp_d, META, META + SEQ), (xs_d, META + SEQ, TX)):
                s, e = max(lo, a), min(hi, b)
                if s < e:
                    out.append((src[s - a:e - a, :], s - lo, e - s))
            return out

        def rows(t):
            return min(P, TY - t * P)

        def xrows(t):
            return min(P, TX - t * P)

        X_COUNT = []
        seen = [0] * 4
        for t in range(XTILES):
            seen[t % 4] += 16 * len(x_rows(t))
            X_COUNT.append(seen[t % 4])

        def n_step(name):
            return STEPS.index(name) + 1

        def n_act(name):
            return BY_ACT.index(name) + 1

        def n_dve(name):
            return BY_DVE.index(name) + 1

        H_OUT = HALVES * HEADS
        H_FFN = H_OUT + 2 * KT
        FFN_ORDER = []
        for p in range(1, 7):
            FFN_ORDER += [("wd", (p - 1) // 2, (p - 1) % 2), ("up", (p + 1) // 2, (p + 1) % 2)]
        FFN_ORDER += [("wd", 3, 0), ("wd", 3, 1), ("next", 0, 0), ("next", 0, 1)]
        NF = len(FFN_ORDER)
        assert NF == 4 * FT

        def ffn_half(kind, a, half):
            return H_FFN + 2 + FFN_ORDER.index((kind, a, half)) if (kind, a) != ("up", 0) else H_FFN + half

        def raw_slot(n):
            m = n - H_OUT
            s = (m + 2) % 4
            return s, m // 4 + (H_OUT // 2 - 1 if s < 2 else 1)

        block = ctx.enter_context(nc.Block())

        @block.sync
        def _(sp):
            def load_x(t):
                if t >= 4:
                    sp.wait_ge(xt_done, t - 3)
                for src, at, n in x_rows(t):
                    sp.dma_start(xr[at:at + n, t % 4, :], src).then_inc(x_in[t % 4], 16)

            def load_in(i, n, slot=None):
                off = UNITS[n // 2][1] + i * P
                s = n % 2 if slot is None else slot
                sp.dma_start(raw[:, s, :].rearrange("p (k c) -> p k c", k=4),
                             w_in_t[:, 4 * (n % 2):4 * (n % 2) + 4, bass.ds(off, P)]).then_inc(raw_in[s], 16)

            def iteration(i, first):
                for n in range(HALVES):
                    if not (first and n < 4):
                        sp.wait_ge(w_split, i * HALVES + n - 1)
                        load_in(i, n)
                    if n == 3:
                        sp.wait_ge(proj_dve, NX + i * 12)
                        sp.dma_start(hc[:, :], c_head[bass.ds(i, 1), :, :].rearrange("a p c -> p (a c)")).then_inc(head_in, 16)
                        sp.dma_start(s_in[:, :], state_ret[0, 0, bass.ds(i, 1), :, :].rearrange("a p c -> p (a c)")).then_inc(head_in, 16)
                        sp.dma_start(gnw[:, :], ret_gn_w[0:1, bass.ds(i * P, P)].rearrange("a p -> p a")).then_inc(head_in, 16)
                        sp.dma_start(cw[:, :], conv_w[0, :, bass.ds(i * P, P)].rearrange("w p -> p w"), allow_slow_non_contiguous=True).then_inc(head_in, 16)
                        sp.dma_start(hist[:, :], state_conv[0, 0, :, bass.ds(i * P, P)].rearrange("w p -> p w"), allow_slow_non_contiguous=True).then_inc(head_in, 16)
                    if n == 9:
                        sp.wait_ge(ret_dve, i * len(BY_DVE) + n_dve("UC"))
                        sp.dma_start(new_ret_sample[0, 0, bass.ds(i, 1), :, :].rearrange("a p c -> p (a c)"), s_new[:, :]).then_inc(s_new_out, 16)
                    if n == 12:
                        sp.wait_ge(ret_dve, i * len(BY_DVE) + n_dve("UB"))
                        sp.dma_start(new_ret_prompt[0, 0, bass.ds(i, 1), :, :].rearrange("a p c -> p (a c)"), st[:, 8 % 5, :]).then_inc(s_end_out, 16)

            load_x(0)
            sp.dma_start(normw[:, :], norm_mix_w[0:1, :].broadcast_to([P, D])).then_inc(const_in, 16)
            sp.dma_start(ident[:, :], c_ident).then_inc(const_in, 16)
            load_x(1)
            load_x(2)
            load_in(0, 0)
            load_in(0, 1)
            load_x(3)
            load_in(0, 2, slot=2)
            load_in(0, 3, slot=3)
            for t in range(4, XTILES):
                load_x(t)
                if t == 5:
                    sp.dma_start(cos_t[:, :], c_cos).then_inc(rope_in, 16)
                    sp.dma_start(sin_t[:, :], c_sin).then_inc(rope_in, 16)
            sp.wait_ge(xn_ready, XTILES)
            iteration(0, True)
            with sp.Fori(1, HEADS) as i:
                iteration(i, False)

            def load_out(m):
                s, _ = raw_slot(H_OUT + m)
                if m >= 2:
                    sp.wait_ge(w_split, H_OUT + m - 3)
                k, nh = KORDER[m // 2], m % 2
                sp.dma_start(raw[:, s, :], w_out_t[:, k, nh * 512:nh * 512 + 512]).then_inc(raw_in[s], 16)

            for m in range(2 * KT):
                load_out(m)
            sp.wait_ge(mix_ready, len(MIX_PARTS) * HEADS)
            sp.wait_ge(s_new_out, 1 + 16 * HEADS)
            sp.wait_ge(s_end_out, 1 + 16 * HEADS)
            sp.dma_start(h[:, 0:2, :], xp_d[0:2 * P, :].rearrange("(t p) n -> p t n", p=P)).then_inc(h_in, 16)
            sp.dma_start(normw[:, :], norm_ffn_w[0:1, :].broadcast_to([P, D])).then_inc(normw_in, 16)
            for w in range(2):
                sp.dma_start(new_conv_prompt[0, 0].rearrange("w (i p) -> p i w", p=P)[:, :, w], ncp[:, :, w],
                             allow_slow_non_contiguous=True).then_inc(conv_out, 16)
                sp.dma_start(new_conv_sample[0, 0].rearrange("w (i p) -> p i w", p=P)[:, :, w], ncs[:, :, w],
                             allow_slow_non_contiguous=True).then_inc(conv_out, 16)
            sp.dma_start(h[:, 2:8, :], xp_d[2 * P:, :].rearrange("(t p) n -> p t n", p=P)).then_inc(h_rest_in, 16)
            sp.wait_ge(conv_out, 64)
            sp.dma_start(h[0:SAMPLE, 8, :], xs_d).then_inc(h_rest_in, 16)

            def load_ffn(g, kind, a, half, n, extra):
                s, _ = raw_slot(n)
                sp.wait_ge(w_split, n - 3 + extra)
                if kind == "wd":
                    src = w_down_t[:, bass.ds(g * FT + a, 1), half * 512:half * 512 + 512].rearrange("p a c -> p (a c)")
                    sp.dma_start(raw[:, s, :], src).then_inc(raw_in[s], 16)
                else:
                    col = (g * FT + a + (FT if kind == "next" else 0)) * P
                    sp.dma_start(raw[:, s, :].rearrange("p (k c) -> p k c", k=4),
                                 w_up_t[:, 4 * half:4 * half + 4, bass.ds(col, P)]).then_inc(raw_in[s], 16)

            def group(g, last):
                for kind, a, half in FFN_ORDER:
                    if not (last and kind == "next"):
                        load_ffn(g, kind, a, half, ffn_half(kind, a, half), g * NF)

            for half in range(2):
                load_ffn(0, "up", 0, half, H_FFN + half, 0)
            with sp.Fori(0, GROUPS - 1) as g:
                group(g, False)
            sp.wait_ge(hw_ready, TILES)
            sp.dma_start(normw[:, :], norm_final_w.rearrange("(a n) -> a n", a=1).broadcast_to([P, D])).then_inc(normw_in, 16)
            group(GROUPS - 1, True)
            for p, t in enumerate(DOWN_ORDER):
                dst = y_prompt[0, t * P:(t + 1) * P, :] if t < SEQ // P else y_sample[0]
                for nh in range(2):
                    sp.wait_ge(y_ready, 2 * p + nh + 1)
                    sl = slice(nh * 512, nh * 512 + 512)
                    sp.dma_start(dst[:, sl], hw[0:rows(t), p % 2, sl]).then_inc(y_out[p % 2], 16)
            sp.wait_ge(y_out[0], 32 * ((TILES + 1) // 2))
            sp.wait_ge(y_out[1], 32 * (TILES // 2))

        @block.scalar
        def _(act):
            def split_in(i, n, first_v=False):
                s = n % 2
                act.wait_ge(raw_in[s], 16 * (i * NU + n // 2 + (1 if first_v else 0)))
                if n >= 2 and s == 0:
                    act.wait_ge(w_used, i * NU + n // 2)
                elif n >= 2:
                    act.wait_ge(proj_done, i * 3 * NU + 3 * (n // 2))
                act.activation(ws_hi[:, s], raw[:, s, :].rearrange("p (k c) -> p k c", k=4), ACT.Copy).then_inc(w_hi, 1)

            def root(t):
                n = xrows(t)
                act.wait_ge(x_in[t % 4], X_COUNT[t])
                if t >= 1:
                    act.wait_ge(ss_ready, t)
                act.activation(junk[0:n, :], xr[0:n, t % 4, :], ACT.Square, accum_out=small[0:n, t % 4, 0:1]).then_inc(ss_ready, 1)
                act.wait_ge(ss_ready, t + 1)
                act.activation(small[0:n, t % 4, 1:2], small[0:n, t % 4, 0:1], ACT.Sqrt, scale=1.0 / D,
                               bias=eps[0:n, :]).then_inc(sd_ready, 1)

            def hi_parts(t):
                n = xrows(t)
                act.wait_ge(xt_done, t + 1)
                for b in range(2):
                    act.activation(hn_hi[:, 4 * b:4 * b + 4, t * P:t * P + n],
                                   ps[T1(t)[b]][:, 0:4 * n].rearrange("p (k c) -> p k c", k=4),
                                   ACT.Copy).then_inc(hn_hi_ready, 1)

            def split_first_k(half):
                act.wait_ge(raw_in[2 + half], 16)
                act.activation(kx_hi[:, half], raw[:, 2 + half, :].rearrange("p (k c) -> p k c", k=4), ACT.Copy).then_inc(w_hi, 1)

            def take_v(i, j, count):
                act.wait_ge(proj_done, count)
                col, n = CGX[j]
                act.activation(vg[:, col:col + n], ps[j][:, 0:n], ACT.Copy).then_inc(proj_act, 1)

            act.wait_ge(eps_ready, 1)
            act.activation(small[:, 3, 3:4], eps[:, :], ACT.Sqrt)
            root(0)
            root(1)
            root(2)
            for t in range(XTILES):
                if t == 1:
                    split_in(0, 0, first_v=True)
                    split_in(0, 1, first_v=True)
                hi_parts(t)
                if 1 <= t < XTILES - 2:
                    root(t + 2)
                if t == 2:
                    split_first_k(0)
                    split_first_k(1)
                if t == 5:
                    take_v(0, 0, 1)
            take_v(0, 1, 3)

            def take_unit(i, uname, j):
                act.wait_ge(proj_done, i * 3 * NU + 3 * [x[0] for x in UNITS].index(uname) + j + 1)
                set0 = [x[0] for x in UNITS].index(uname) % 2 * 3
                col, n = dict((x[0], x[2]) for x in UNITS)[uname][j]
                bank = ps[set0 + j]
                if uname == "v":
                    if j == 0:
                        act.wait_ge(proj_dve, NX + i * 12)
                    take_v(i, j, i * 3 * NU + j + 1)
                elif uname == "g":
                    if j == 0:
                        act.wait_ge(ret_done, i * NS + n_step("vC"))
                    act.activation(vg[:, col:col + n], bank[:, 0:n], ACT.Silu).then_inc(proj_act, 1)
                else:
                    if j == 0:
                        act.wait_ge(proj_dve, NX + i * 12)
                    if j < 2:
                        act.activation(u[:, col:col + n], bank[:, 0:n], ACT.Copy).then_inc(proj_act, 1)
                    else:
                        m = META + SEQ - col
                        act.activation(u[:, col:col + m], bank[:, 0:m], ACT.Copy)
                        act.activation(u[:, col + m + 2:TX + 2], bank[:, m:n], ACT.Copy).then_inc(proj_act, 1)

            def take_step(i, name):
                bank = ps[RET[STEPS.index(name) % 2]]
                if name in BY_ACT:
                    act.wait_ge(ret_done, i * NS + n_step(name))
                if name in ("vA", "vB"):
                    c = 0 if name == "vA" else 4
                    act.activation(v_tok[:, c:c + 4, :], bank[:, :].rearrange("p (c e) -> p c e", c=4), ACT.Copy).then_inc(ret_act, 1)
                elif name == "vC":
                    act.activation(v_tok[0:META, 8, :], bank[0:META, 0:HD], ACT.Copy)
                    act.activation(v_tok[0:SAMPLE, 9, :], bank[0:SAMPLE, HD:2 * HD], ACT.Copy).then_inc(ret_act, 1)
                elif name == "kC":
                    act.wait_ge(head_in, 16 * 5 * (i + 1))
                    act.activation(kdC[0:META, 0, :], bank[0:META, 0:HD], ACT.Copy, scale=hc[0:META, C_KMETA:C_KMETA + 1])
                    act.activation(kdC[0:SAMPLE, 1, :], bank[0:SAMPLE, HD:2 * HD], ACT.Copy,
                                   scale=hc[0:SAMPLE, C_KSAMP:C_KSAMP + 1]).then_inc(ret_act, 1)
                elif name in ("kA", "kB"):
                    act.activation(kd[:, :, :], bank[:, :].rearrange("p (c e) -> p c e", c=4), ACT.Copy,
                                   scale=hc[:, C_KDEC:C_KDEC + 1]).then_inc(ret_act, 1)
                elif name in ("oC", "oA", "oB"):
                    w, n = (1, SAMPLE) if name == "oC" else (4, P)
                    act.wait_ge(var_ready, i * 3 + ["oC", "oA", "oB"].index(name) + 1)
                    act.activation(small[0:n, 1, 0:w], small[0:n, 0, 0:w], ACT.Sqrt).then_inc(gsd_ready, 1)
                elif name in ("tC", "tA", "tB"):
                    act.wait_ge(ret_dve, i * len(BY_DVE) + n_dve(name))
                    col, n = {"tC": (SEQ, SAMPLE), "tA": (0, 512), "tB": (512, 512)}[name]
                    src = onC[:, 0:SAMPLE] if name == "tC" else on[:, :, :].rearrange("p c e -> p (c e)")
                    act.activation(mid_hi[:, bass.ds(i + 4, 1), col:col + n].rearrange("p a c -> p (a c)"), src, ACT.Copy).then_inc(mix_hi_ready, 1)

            def tap0(i):
                act.wait_ge(proj_dve, NX + i * 12 + 9)
                act.wait_ge(head_in, 16 * 5 * (i + 1))
                act.activation(u[:, META + SEQ:META + SEQ + 2], hist[:, :], ACT.Copy).then_inc(act_step, 1)
                act.wait_ge(act_step, i + 1)
                for a, w, s in CONV:
                    last = act.activation(y[:, a:a + w], u[:, s:s + w], ACT.Copy, scale=cw[:, 0:1])
                last.then_inc(tap0_ready, 1)

            def conv_hi(i, j):
                act.wait_ge(proj_dve, NX + i * 12 + 9 + j + 1)
                col, n = CGQ[j]
                act.activation(mid_hi[:, bass.ds(i, 1), col - META:col - META + n].rearrange("p a c -> p (a c)"),
                               y[:, col - META:col - META + n], ACT.Copy).then_inc(mix_hi_ready, 1)

            def split_out(m):
                s, before = raw_slot(H_OUT + m)
                act.wait_ge(raw_in[s], 16 * (before + 1))
                act.activation(wo_hi[:, m // 2, m % 2 * 512:m % 2 * 512 + 512], raw[:, s, :], ACT.Copy).then_inc(w_hi, 1)

            def iteration(i, first, last):
                after = AFTER_FIRST if first else AFTER
                for un in range(2 if first else 0, NU):
                    for b in range(6):
                        half = 2 * un + b // 3
                        if b % 3 == 0 and half >= 1 and not (last and half + 1 == HALVES):
                            split_in(i, half + 1)
                        if b >= 3 and UNITS[un][0] in ACT_UNITS:
                            take_unit(i, UNITS[un][0], b - 3)
                        if b >= 3 and UNITS[un][0] == "b":
                            conv_hi(i, b - 3)
                        if (un, b) in after:
                            take_step(i, after[un, b])
                        if (un, b) == (5, 5):
                            tap0(i)
                        if last and un == NU - 1 and b in (3, 4):
                            if b == 3:
                                act.wait_ge(w_used, NU * HEADS)
                            split_out(2 * b - 6)
                            split_out(2 * b - 5)
                if not last:
                    split_in(i, HALVES + 1)

            take_v(0, 2, 5)
            split_in(0, 4)
            iteration(0, True, False)
            with act.Fori(1, HEADS - 1) as i:
                iteration(i, False, False)
            iteration(HEADS - 1, False, True)

            for m in range(4, 2 * KT):
                if m == 8:
                    act.wait_ge(proj_done, 3 * NU * HEADS)
                split_out(m)

            def ht_hi(t):
                n = rows(t)
                act.wait_ge(ht_done, t + 1)
                for b in range(2):
                    act.activation(mid_hi[:, 4 * b:4 * b + 4, t * P:t * P + n],
                                   ps[T3(t)[b]][:, 0:4 * n].rearrange("p (k c) -> p k c", k=4),
                                   ACT.Copy).then_inc(ht_hi_ready, 1)

            def split_ffn(g, kind, a, half):
                n = ffn_half(kind, a, half)
                s, before = raw_slot(n)
                act.wait_ge(raw_in[s], 16 * (before + 1) + g * (16 * NF // 4))
                if kind == "wd":
                    act.activation(wd_hi[:, a, half * 512:half * 512 + 512], raw[:, s, :], ACT.Copy).then_inc(w_hi, 1)
                else:
                    act.activation(ws_hi[:, half], raw[:, s, :].rearrange("p (k c) -> p k c", k=4), ACT.Copy).then_inc(w_hi, 1)

            for t in range(TILES):
                ht_hi(t)
                if t == 2:
                    split_ffn(0, "up", 0, 0)
                    split_ffn(0, "up", 0, 1)

            rl_flat = rl[:, :, :].rearrange("p s c -> p (s c)")[:, 0:512]

            def group(g, last):
                for p in range(8):
                    if 1 <= p:
                        if p % 2 == 1:
                            act.wait_ge(w_used, NU * HEADS + FT * g + p // 2 + 1)
                        else:
                            act.wait_ge(up_done, 12 * g + 3 * (p // 2))
                        split_ffn(g, *FFN_ORDER[2 * p - 2])
                        split_ffn(g, *FFN_ORDER[2 * p - 1])
                    if p % 2 == 1:
                        a = p // 2
                        for j in range(3):
                            n = 3 * a + j
                            w = CGY[j][1]
                            act.wait_ge(up_done, 12 * g + n + 1)
                            act.activation(rl[:, n % 2, 0:w], ps[a % 2 * 3 + j][:, 0:w], ACT.Relu).then_inc(relu_done, 1)
                            act.wait_ge(sq_done, 12 * g + n + 1)
                            act.activation(f_hi[:, a, CGY[j][0]:CGY[j][0] + w], sq[:, n % 2, 0:w], ACT.Copy).then_inc(f_hi_ready, 1)
                if not last:
                    act.wait_ge(up_done, 12 * g + 12)
                    split_ffn(g, "next", 0, 0)
                    split_ffn(g, "next", 0, 1)
                else:
                    for p, t in enumerate(DOWN_ORDER):
                        n = rows(t)
                        s0, s1, part, sd = (small[0:n, p % 4, x:x + 1] for x in range(4))
                        act.wait_ge(fin_half, p + 1)
                        if p:
                            act.wait_ge(fin_step, 3 * p)
                        act.activation(rl_flat[0:n, :], h[0:n, t, 0:512], ACT.Square, accum_out=s0).then_inc(fin_step, 1)
                        act.wait_ge(fin_step, 3 * p + 1)
                        act.activation(part, s0, ACT.Identity, scale=1.0 / D, bias=eps[0:n, :]).then_inc(fin_step, 1)
                        act.wait_ge(down_taken, 2 + 9 * g + p + 1)
                        act.activation(rl_flat[0:n, :], h[0:n, t, 512:1024], ACT.Square, accum_out=s1).then_inc(fin_step, 1)
                        act.wait_ge(fin_step, 3 * p + 3)
                        act.activation(sd, s1, ACT.Sqrt, scale=1.0 / D, bias=part).then_inc(fin_sd, 1)

            with act.Fori(0, GROUPS - 1) as g:
                group(g, False)
            group(GROUPS - 1, True)

        @block.vector
        def _(dve):
            chain = {"n": 0, "base": 0}

            def link(ins):
                chain["n"] += 1
                ins.then_inc(dve_step, 1)
                dve.wait_ge(dve_step, chain["n"] + chain["base"])

            def mean_square(src, n, slot):
                dve.bn_stats(bn[0:n, 0, :], src[:, 0:512])
                link(dve.bn_stats(bn[0:n, 1, :], src[:, 512:1024]))
                link(dve.bn_aggr(mv[0:n, :], bn[0:n, 0:2, :]))
                link(dve.scalar_tensor_tensor(small[0:n, slot, 0:1], mv[0:n, 0:1], mv[0:n, 0:1], mv[0:n, 1:2], ALU.mult, ALU.add))
                return dve.tensor_scalar(small[0:n, slot, 0:1], small[0:n, slot, 0:1], EPS, None, ALU.add)

            def split_in(i, n):
                dve.wait_ge(w_hi, i * HALVES + n + 1)
                s = n % 2
                dve.tensor_tensor(ws_lo[:, s], raw[:, s, :].rearrange("p (k c) -> p k c", k=4),
                                  ws_hi[:, s].bitcast(F32), ALU.subtract).then_inc(w_split, 1)

            dve.sem_inc(proj_dve, NX)
            dve.sem_inc(down_taken, 2)
            dve.sem_inc(s_new_out, 1)
            dve.sem_inc(s_end_out, 1)
            dve.memset(eps[:, :], EPS).then_inc(eps_ready, 1)
            dve.memset(on[:, :, :], 0.0).then_inc(warm_ready, 1)
            dve.wait_ge(const_in, 32)

            def normed(t):
                n = xrows(t)
                dve.wait_ge(sd_ready, t + 1)
                link(dve.reciprocal(small[0:n, t % 4, 2:3], small[0:n, t % 4, 1:2]))
                dve.scalar_tensor_tensor(xr[0:n, t % 4, :], xr[0:n, t % 4, :], small[0:n, t % 4, 2:3], normw[0:n, :],
                                         ALU.mult, ALU.mult).then_inc(xn_ready, 1)

            def lo_parts(t):
                n = xrows(t)
                for b in range(2):
                    dve.wait_ge(hn_hi_ready, 2 * t + b + 1)
                    sl = (slice(None), slice(4 * b, 4 * b + 4), slice(t * P, t * P + n))
                    last = dve.tensor_tensor(hn_lo[sl], ps[T1(t)[b]][:, 0:4 * n].rearrange("p (k c) -> p k c", k=4),
                                             hn_hi[sl].bitcast(F32), ALU.subtract)
                last.then_inc(hn_ready, 1)

            def split_first_k(half):
                dve.wait_ge(w_hi, 3 + half)
                dve.tensor_tensor(kx_lo[:, half], raw[:, 2 + half, :].rearrange("p (k c) -> p k c", k=4),
                                  kx_hi[:, half].bitcast(F32), ALU.subtract).then_inc(w_split, 1)

            link(dve.memset(onC[:, :], 0.0))

            names = [x[0] for x in UNITS]

            def rotary(dst, bank, col, n, at, before):
                dve.tensor_tensor(dst[:, at:at + n], bank[:, 0:n], cos_t[:, col:col + n], ALU.mult)
                dve.wait_ge(proj_dve, before)
                dve.tensor_tensor(rot[0:64, 0:n], bank[64:128, 0:n], sin_t[0:64, col:col + n], ALU.mult)
                link(dve.tensor_tensor(rot[64:128, 0:n], bank[0:64, 0:n], sin_t[64:128, col:col + n], ALU.mult))
                return dve.tensor_tensor(dst[:, at:at + n], dst[:, at:at + n], rot[:, 0:n], ALU.add)

            for t in range(3):
                normed(t)
            for t in range(XTILES):
                if 3 <= t < XTILES - 1:
                    normed(t + 1)
                lo_parts(t)
                if t == 0:
                    split_in(0, 0)
                    split_in(0, 1)
                if t == 2:
                    normed(3)
                if t == 2:
                    split_first_k(0)
                    split_first_k(1)
                    dve.wait_ge(rope_in, 32)
                if t == 5:
                    dve.wait_ge(proj_done, 2)
                    rotary(kT, ps[3], *CGX[0], CGX[0][0], NX).then_inc(proj_dve, 1)
            dve.wait_ge(proj_done, 4)
            rotary(kT, ps[4], *CGX[1], CGX[1][0], NX + 1).then_inc(proj_dve, 1)
            split_in(0, 4)
            dve.wait_ge(proj_done, 6)
            rotary(kT, ps[5], *CGX[2], CGX[2][0], NX + 2).then_inc(proj_dve, 1)

            def mix_lo(k, dst, at, src, col, n):
                hi = mid_hi[:, bass.ds(k, 1), col:col + n].rearrange("p a c -> p (a c)").bitcast(F32)
                return dve.tensor_tensor(dst[:, bass.ds(k, 1), at:at + n].rearrange("p a c -> p (a c)"), src, hi, ALU.subtract)

            def take_unit(i, uname, j):
                un = names.index(uname)
                dve.wait_ge(proj_done, i * 3 * NU + 3 * un + j + 1)
                bank = ps[un % 2 * 3 + j]
                col, n = UNITS[un][2][j]
                if uname == "k":
                    rotary(kT, bank, col, n, col, NX + i * 12 + j).then_inc(proj_dve, 1)
                elif uname == "q":
                    rotary(qT, bank, col, n, col - META, NX + i * 12 + 3 + j).then_inc(proj_dve, 1)
                elif uname == "c":
                    dve.wait_ge(proj_act, i * 9 + 6 + j + 1)
                    m = min(n, META + SEQ - col)
                    ins = dve.tensor_tensor(u[:, col:col + m], bank[:, 0:m], u[:, col:col + m], ALU.mult)
                    if m < n:
                        ins = dve.tensor_tensor(u[:, col + m + 2:TX + 2], bank[:, m:n], u[:, col + m + 2:TX + 2], ALU.mult)
                    ins.then_inc(proj_dve, 1)
                else:
                    a = col - META
                    dve.tensor_tensor(y[:, a:a + n], bank[:, 0:n], y[:, a:a + n], ALU.mult).then_inc(proj_dve, 1)
                    dve.wait_ge(mix_hi_ready, i * 6 + 3 + j + 1)
                    m = min(n, SEQ - a)
                    ins = mix_lo(i, mid_lo, a, y[:, a:a + m], a, m)
                    if m < n:
                        ins = mix_lo(i, mid_hi, TY, y[:, SEQ:TY], SEQ, SAMPLE)
                    ins.then_inc(mix_ready, 1)

            def conv(i):
                dve.wait_ge(tap0_ready, i + 1)
                dve.tensor_copy(ncp[:, bass.ds(i, 1), :].rearrange("p a c -> p (a c)"), u[:, META + SEQ - 2:META + SEQ])
                dve.tensor_copy(ncs[:, bass.ds(i, 1), :].rearrange("p a c -> p (a c)"), u[:, TX:TX + 2])
                for tap in (1, 2):
                    for a, w, s in CONV:
                        ins = dve.scalar_tensor_tensor(y[:, a:a + w], u[:, s + tap:s + tap + w], cw[:, tap:tap + 1],
                                                       y[:, a:a + w], ALU.mult, ALU.add)
                    link(ins)

            def take_step(i, name):
                bank = ps[RET[STEPS.index(name) % 2]]
                dve.wait_ge(ret_done, i * NS + n_step(name))
                if name == "UC":
                    dve.wait_ge(head_in, 16 * 5 * (i + 1))
                    dve.wait_ge(s_new_out, 1 + 16 * i)
                    dve.tensor_copy(st[:, 0, :], bank[:, 0:HD])
                    dve.scalar_tensor_tensor(s_new[:, :], s_in[:, :], hc[:, C_G64:C_G64 + 1], bank[:, HD:2 * HD],
                                             ALU.mult, ALU.add).then_inc(ret_dve, 1)
                elif name in ("UA", "UB"):
                    if name == "UA":
                        dve.wait_ge(s_end_out, 1 + 16 * i)
                    c0 = 0 if name == "UA" else 4
                    for c in range(c0, c0 + 4):
                        ins = dve.scalar_tensor_tensor(st[:, (c + 1) % 5, :], st[:, c % 5, :], hc[:, C_G128:C_G128 + 1],
                                                       bank[:, (c - c0) * HD:(c - c0 + 1) * HD], ALU.mult, ALU.add)
                        if c < c0 + 3:
                            link(ins)
                    ins.then_inc(ret_dve, 1)
                elif name == "sC":
                    dve.tensor_tensor(smC[0:SAMPLE, :], bank[0:SAMPLE, 0:SAMPLE], hc[0:SAMPLE, 0:SAMPLE], ALU.mult).then_inc(ret_dve, 1)
                elif name in ("sA", "sB"):
                    mask = hc[:, 0:P].rearrange("p (a j) -> p a j", a=1).broadcast_to([P, 4, P])
                    dve.tensor_tensor(sm[:, :, :], bank[:, :].rearrange("p (c j) -> p c j", c=4), mask, ALU.mult).then_inc(ret_dve, 1)
                elif name in ("oC", "oA", "oB"):
                    w, n = (1, SAMPLE) if name == "oC" else (4, P)
                    for c in range(w):
                        ins = dve.bn_stats(bn[0:n, c, :], bank[0:n, c * HD:(c + 1) * HD])
                    link(ins)
                    m_even, s_even, m_odd, s_odd = (bn[0:n, 0:w, x] for x in (1, 2, 4, 5))
                    mean, diff, tot = (gs[0:n, x, 0:w] for x in range(3))
                    dve.tensor_tensor(mean, m_even, m_odd, ALU.add)
                    dve.tensor_tensor(diff, m_even, m_odd, ALU.subtract)
                    link(dve.tensor_tensor(tot, s_even, s_odd, ALU.add))
                    dve.tensor_scalar(mean, mean, 0.5, None, ALU.mult)
                    link(dve.scalar_tensor_tensor(diff, diff, 0.25, diff, ALU.mult, ALU.mult))
                    link(dve.scalar_tensor_tensor(tot, tot, 1.0 / HD, diff, ALU.mult, ALU.add))
                    ins = dve.tensor_scalar(small[0:n, 0, 0:w], tot, hc[0:n, C_C2:C_C2 + 1], GN_EPS, ALU.mult, ALU.add)
                    ins.then_inc(var_ready, 1)
                    dve.wait_ge(gsd_ready, i * 3 + ["oC", "oA", "oB"].index(name) + 1)
                    link(dve.reciprocal(small[0:n, 2, 0:w], small[0:n, 1, 0:w]))
                    link(dve.tensor_scalar(small[0:n, 3, 0:w], small[0:n, 2, 0:w], hc[0:n, C_C:C_C + 1], None, ALU.mult))
                    for c in range(w):
                        dst = onC[0:n, :] if name == "oC" else on[:, c, :]
                        ins = dve.tensor_scalar(dst, bank[0:n, c * HD:(c + 1) * HD], gs[0:n, 0, c:c + 1], small[0:n, 3, c:c + 1],
                                                ALU.subtract, ALU.mult)
                    ins.then_inc(ret_dve, 1)
                elif name in ("tC", "tA", "tB"):
                    dve.wait_ge(proj_act, i * 9 + 6)
                    col, n = {"tC": (SEQ, SAMPLE), "tA": (0, 512), "tB": (512, 512)}[name]
                    og = onC[:, 0:SAMPLE] if name == "tC" else on[:, :, :].rearrange("p c e -> p (c e)")
                    dve.scalar_tensor_tensor(og, bank[:, 0:n], gnw[:, 0:1], vg[:, META + col:META + col + n],
                                             ALU.mult, ALU.mult).then_inc(ret_dve, 1)
                    dve.wait_ge(mix_hi_ready, i * 6 + MIX_PARTS.index(name) + 1)
                    dst, at = (mid_hi, TY) if name == "tC" else (mid_lo, col)
                    mix_lo(i + 4, dst, at, og, col, n).then_inc(mix_ready, 1)

            def split_out(m):
                dve.wait_ge(w_hi, H_OUT + m + 1)
                s, _ = raw_slot(H_OUT + m)
                sl = (slice(None), m // 2, slice(m % 2 * 512, m % 2 * 512 + 512))
                dve.tensor_tensor(wo_lo[sl], raw[:, s, :], wo_hi[sl].bitcast(F32), ALU.subtract).then_inc(w_split, 1)

            def iteration(i, first, last):
                after = AFTER_FIRST if first else AFTER
                for un in range(2 if first else 0, NU):
                    for b in range(6):
                        half = 2 * un + b // 3
                        if b % 3 == 0 and half >= 1 and not (last and half + 1 == HALVES):
                            split_in(i, half + 1)
                        if (un, b) == (NU - 1, 0):
                            conv(i)
                        if b >= 3 and names[un] in DVE_UNITS:
                            take_unit(i, names[un], b - 3)
                        if (un, b) in after and after[un, b] in BY_DVE:
                            take_step(i, after[un, b])
                        if last and un == NU - 1 and b in (3, 4):
                            split_out(2 * b - 6)
                            split_out(2 * b - 5)
                if not last:
                    split_in(i, HALVES + 1)

            LINKS = 32
            iteration(0, True, False)
            start = chain["n"]
            with dve.Fori(1, HEADS - 1) as i:
                chain["base"] = (i - 1) * LINKS
                iteration(i, False, False)
            assert chain["n"] == start + LINKS, chain["n"] - start
            chain.update(n=start + (HEADS - 2) * LINKS, base=0)
            iteration(HEADS - 1, False, True)

            for m in range(4, 2 * KT):
                split_out(m)
            dve.wait_ge(normw_in, 16)

            def residual(t):
                n = rows(t)
                dve.wait_ge(out_done, t + 1)
                if t == 0:
                    dve.wait_ge(h_in, 16)
                if t == 2:
                    dve.wait_ge(h_rest_in, 32)
                pair = OUT_PAIRS[t % 2]
                for nh in range(2):
                    sl = slice(nh * 512, nh * 512 + 512)
                    ins = dve.tensor_tensor(h[0:n, t, sl], ps[pair[nh]][0:n, :], h[0:n, t, sl], ALU.add)
                    if t == TILES - 1:
                        link(ins)
                        ins = dve.tensor_tensor(h[0:n, t, sl], ps[pair[nh]][n:2 * n, :], h[0:n, t, sl], ALU.add)
                ins.then_inc(out_taken, 1)
                dve.wait_ge(out_taken, t + 1)
                if t >= 2:
                    dve.wait_ge(ht_done, t - 1)
                dve.tensor_tensor(hw[0:n, t % 2, :], h[0:n, t, :], normw[0:n, :], ALU.mult).then_inc(hw_ready, 1)

            def inverse_ms(t):
                n = rows(t)
                link(mean_square(h[0:n, t, :], n, 0))
                dve.reciprocal(inv_ms[0:n, t:t + 1], small[0:n, 0, 0:1]).then_inc(ms2_ready, 1)

            def ht_lo(t):
                n = rows(t)
                for b in range(2):
                    dve.wait_ge(ht_hi_ready, 2 * t + b + 1)
                    sl = (slice(None), slice(4 * b, 4 * b + 4), slice(t * P, t * P + n))
                    last = dve.tensor_tensor(mid_lo[sl], ps[T3(t)[b]][:, 0:4 * n].rearrange("p (k c) -> p k c", k=4),
                                             mid_hi[sl].bitcast(F32), ALU.subtract)
                last.then_inc(ht_ready, 1)

            def split_ffn(g, kind, a, half):
                n = ffn_half(kind, a, half)
                s, _ = raw_slot(n)
                dve.wait_ge(w_hi, n + 1 + g * NF)
                if kind == "wd":
                    sl = (slice(None), a, slice(half * 512, half * 512 + 512))
                    dve.tensor_tensor(wd_lo[sl], raw[:, s, :], wd_hi[sl].bitcast(F32), ALU.subtract).then_inc(w_split, 1)
                else:
                    dve.tensor_tensor(ws_lo[:, half], raw[:, s, :].rearrange("p (k c) -> p k c", k=4),
                                      ws_hi[:, half].bitcast(F32), ALU.subtract).then_inc(w_split, 1)

            residual(0)
            residual(1)
            inverse_ms(0)
            inverse_ms(1)
            ht_lo(0)
            ht_lo(1)
            for t in range(2, TILES):
                residual(t)
                if t == 3:
                    split_ffn(0, "up", 0, 0)
                    split_ffn(0, "up", 0, 1)
                if t < TILES - 1:
                    inverse_ms(t)
                ht_lo(t)
            inverse_ms(TILES - 1)

            def take_down(g, p, last):
                t = DOWN_ORDER[p]
                n = rows(t)
                pair = DOWN_PAIRS[p % 3]
                for nh in range(2):
                    sl = slice(nh * 512, nh * 512 + 512)
                    dve.wait_ge(down_done, 2 * (9 * g + p) + nh + 1)
                    ins = dve.scalar_tensor_tensor(h[0:n, t, sl], ps[pair[nh]][0:n, :], inv_ms[0:n, t:t + 1], h[0:n, t, sl],
                                                   ALU.mult, ALU.add)
                    if t == TILES - 1:
                        link(ins)
                        ins = dve.scalar_tensor_tensor(h[0:n, t, sl], ps[pair[nh]][n:2 * n, :], inv_ms[0:n, t:t + 1],
                                                       h[0:n, t, sl], ALU.mult, ALU.add)
                    if last and nh == 0:
                        ins.then_inc(fin_half, 1)
                ins.then_inc(down_taken, 1)

            def final_norm(p):
                t = DOWN_ORDER[p]
                n = rows(t)
                dve.wait_ge(fin_sd, p + 1)
                link(dve.reciprocal(small[0:n, p % 4, 0:1], small[0:n, p % 4, 3:4]))
                if p >= 2:
                    dve.wait_ge(y_out[p % 2], 32 * (p // 2))
                for nh in range(2):
                    sl = slice(nh * 512, nh * 512 + 512)
                    dve.scalar_tensor_tensor(hw[0:n, p % 2, sl], h[0:n, t, sl], small[0:n, p % 4, 0:1],
                                             normw[0:n, sl], ALU.mult, ALU.mult).then_inc(y_ready, 1)

            def group(g, last):
                for p in range(8):
                    if 1 <= p:
                        split_ffn(g, *FFN_ORDER[2 * p - 2])
                        split_ffn(g, *FFN_ORDER[2 * p - 1])
                    if p % 2 == 1:
                        a = p // 2
                        for j in range(3):
                            n = 3 * a + j
                            w = CGY[j][1]
                            col, m = CGY[j][0], min(w, SEQ - CGY[j][0])
                            dve.wait_ge(relu_done, 12 * g + n + 1)
                            dve.tensor_tensor(sq[:, n % 2, 0:w], rl[:, n % 2, 0:w], rl[:, n % 2, 0:w], ALU.mult).then_inc(sq_done, 1)
                            dve.wait_ge(f_hi_ready, 12 * g + n + 1)
                            ins = dve.tensor_tensor(f_lo[:, a, col:col + m], sq[:, n % 2, 0:m],
                                                    f_hi[:, a, col:col + m].bitcast(F32), ALU.subtract)
                            if m < w:
                                ins = dve.tensor_tensor(f_hi[:, a, TY:TP], sq[:, n % 2, m:w], f_hi[:, a, SEQ:TY].bitcast(F32), ALU.subtract)
                            ins.then_inc(f_ready, 1)
                if not last:
                    split_ffn(g, "next", 0, 0)
                    split_ffn(g, "next", 0, 1)
                for p in range(TILES):
                    take_down(g, p, last)
                    if last and p >= 1:
                        final_norm(p - 1)
                if last:
                    final_norm(TILES - 1)

            start = chain["n"]
            with dve.Fori(0, GROUPS - 1) as g:
                chain["base"] = g * 2
                group(g, False)
            assert chain["n"] == start + 2
            chain.update(n=start + (GROUPS - 1) * 2, base=0)
            dve.wait_ge(normw_in, 32)
            group(GROUPS - 1, True)

        @block.tensor
        def _(pe):
            def passes(out, a_hi, a_lo, b_hi, b_lo, start, stop):
                pe.matmul(out, a_hi, b_hi, start=start, stop=False)
                pe.matmul(out, a_hi, b_lo, start=False, stop=False)
                return pe.matmul(out, a_lo, b_hi, start=False, stop=stop)

            def passes_sample(out, a_hi_lo, b_hi, b_lo, start, stop):
                pe.matmul(out, a_hi_lo, b_hi, start=start, stop=False)
                return pe.matmul(out, a_hi_lo, b_lo, start=False, stop=stop)

            def transposed_x(t):
                n = xrows(t)
                pe.wait_ge(xn_ready, t + 1)
                if t >= 3:
                    pe.wait_ge(hn_ready, t - 1)
                for k in range(KT):
                    last = pe.transpose(ps[T1(t)[k // 4]][:, k % 4 * n:k % 4 * n + n],
                                        xr[0:n, t % 4, k * P:(k + 1) * P], ident[0:n, 0:n])
                last.then_inc(xt_done, 1)

            def keep_warm(times):
                for n in range(times):
                    pe.matmul(ps[0][:, :], on[:, 0, :], on[:, :, :].rearrange("p c e -> p (c e)"), start=True, stop=True)

            pe.wait_ge(warm_ready, 1)
            keep_warm(3)
            pe.wait_ge(const_in, 32)
            for t in range(3):
                transposed_x(t)
                keep_warm([2, 0, 3][t])
            for j, (col, w) in enumerate(CGX):
                pe.wait_ge(hn_ready, 3 * (j + 1))
                for un, (a_hi, a_lo) in enumerate(((ws_hi, ws_lo), (kx_hi, kx_lo))):
                    for half in range(2):
                        pe.wait_ge(w_split, 2 * un + half + 1)
                        for k in range(4):
                            kk = 4 * half + k
                            last = passes(ps[3 * un + j][:, 0:w], a_hi[:, half, k, :], a_lo[:, half, k, :],
                                          hn_hi[:, kk, col:col + w], hn_lo[:, kk, col:col + w],
                                          start=kk == 0, stop=kk == KT - 1)
                        if half == 1:
                            last.then_inc(proj_done, 1)
                        elif j == 2:
                            last.then_inc(w_used, 1)
                        if j < 2 and 2 * un + half < 3:
                            transposed_x(3 * (j + 1) + 2 * un + half)

            names = [x[0] for x in UNITS]

            def bank_free(i, un, j):
                name = names[un]
                if name == "v":
                    pe.wait_ge(proj_dve, i * 12 + j + 1)
                elif name == "q":
                    pe.wait_ge(proj_act, i * 9 + j + 1)
                elif name == "g":
                    pe.wait_ge(proj_dve, NX + i * 12 + j + 1)
                elif name == "xt":
                    pe.wait_ge(proj_dve, NX + i * 12 + 3 + j + 1)
                elif name == "c":
                    pe.wait_ge(proj_act, i * 9 + 3 + j + 1)
                elif name == "b":
                    pe.wait_ge(proj_act, i * 9 + 6 + j + 1)

            def step(i, name):
                s = STEPS.index(name)
                out = ps[RET[s % 2]]
                if s < 2:
                    pe.wait_ge(proj_dve, NX + i * 12)
                elif STEPS[s - 2] in BY_ACT:
                    pe.wait_ge(ret_act, i * len(BY_ACT) + n_act(STEPS[s - 2]))
                else:
                    pe.wait_ge(ret_dve, i * len(BY_DVE) + n_dve(STEPS[s - 2]))
                c0 = 4 if name[1] == "B" else 0
                if name[0] in "vk" and name[1] in "AB":
                    src = vg if name[0] == "v" else kT
                    if name[0] == "v":
                        pe.wait_ge(proj_act, i * 9 + (2 if name == "vA" else 3))
                    for c in range(4):
                        at = META + (c0 + c) * P
                        last = pe.transpose(out[:, c * P:(c + 1) * P], src[:, at:at + P], ident[:, :])
                elif name in ("vC", "kC"):
                    src = vg if name == "vC" else kT
                    if name == "kC":
                        pe.wait_ge(proj_dve, NX + i * 12 + 3)
                    pe.transpose(out[0:META, 0:HD], src[:, 0:META], ident[:, :])
                    last = pe.transpose(out[0:SAMPLE, HD:2 * HD], src[:, META + SEQ:TX], ident[:, :])
                elif name == "UC":
                    pe.wait_ge(ret_act, i * len(BY_ACT) + n_act("kC"))
                    pe.matmul(out[:, 0:HD], kdC[0:META, 0, :], v_tok[0:META, 8, :], start=True, stop=True)
                    last = pe.matmul(out[:, HD:2 * HD], kdC[0:SAMPLE, 1, :], v_tok[0:SAMPLE, 9, :], start=True, stop=True)
                elif name in ("UA", "UB"):
                    pe.wait_ge(ret_act, i * len(BY_ACT) + n_act("kA" if name == "UA" else "kB"))
                    for c in range(4):
                        last = pe.matmul(out[:, c * HD:(c + 1) * HD], kd[:, c, :], v_tok[:, c0 + c, :], start=True, stop=True)
                elif name == "sC":
                    pe.wait_ge(proj_dve, NX + i * 12 + 6)
                    last = pe.matmul(out[0:SAMPLE, 0:SAMPLE], kT[:, META + SEQ:TX], qT[:, SEQ:TY], start=True, stop=True)
                elif name in ("sA", "sB"):
                    for c in range(4):
                        at = (c0 + c) * P
                        last = pe.matmul(out[:, c * P:(c + 1) * P], kT[:, META + at:META + at + P], qT[:, at:at + P], start=True, stop=True)
                elif name == "oC":
                    pe.wait_ge(ret_dve, i * len(BY_DVE) + n_dve("sC"))
                    pe.wait_ge(head_in, 16 * 5 * (i + 1))
                    pe.matmul(out[0:SAMPLE, 0:HD], qT[:, SEQ:TY], s_in[:, :], start=True, stop=False)
                    last = pe.matmul(out[0:SAMPLE, 0:HD], smC[0:SAMPLE, :], v_tok[0:SAMPLE, 9, :], start=False, stop=True)
                elif name in ("oA", "oB"):
                    pe.wait_ge(ret_dve, i * len(BY_DVE) + n_dve("sA" if name == "oA" else "sB"))
                    for c in range(4):
                        at = (c0 + c) * P
                        pe.matmul(out[:, c * HD:(c + 1) * HD], sm[:, c, :], v_tok[:, c0 + c, :], start=True, stop=False)
                        last = pe.matmul(out[:, c * HD:(c + 1) * HD], qT[:, at:at + P], st[:, (c0 + c) % 5, :], start=False, stop=True)
                elif name == "tC":
                    last = pe.transpose(out[:, 0:P], onC[:, :], ident[:, :])
                else:
                    pe.wait_ge(ret_dve, i * len(BY_DVE) + n_dve("oA" if name == "tA" else "oB"))
                    for c in range(4):
                        last = pe.transpose(out[:, c * P:(c + 1) * P], on[:, c, :], ident[:, :])
                last.then_inc(ret_done, 1)

            def iteration(i, first):
                after = AFTER_FIRST if first else AFTER
                for un in range(2 if first else 0, NU):
                    groups = UNITS[un][2]
                    for half in range(2):
                        n = 2 * un + half
                        pe.wait_ge(w_split, i * HALVES + n + 1)
                        for j, (col, w) in enumerate(groups):
                            if half == 0:
                                bank_free(i, un, j)
                            out = ps[un % 2 * 3 + j][:, 0:w]
                            for k in range(4):
                                kk = 4 * half + k
                                last = passes(out, ws_hi[:, n % 2, k, :], ws_lo[:, n % 2, k, :],
                                              hn_hi[:, kk, col:col + w], hn_lo[:, kk, col:col + w],
                                              start=kk == 0, stop=kk == KT - 1)
                            if half == 1:
                                last.then_inc(proj_done, 1)
                            if (un, 3 * half + j) in after and j < 2:
                                step(i, after[un, 3 * half + j])
                        if half == 0:
                            last.then_inc(w_used, 1)
                        if (un, 3 * half + 2) in after:
                            step(i, after[un, 3 * half + 2])

            iteration(0, True)
            with pe.Fori(1, HEADS) as i:
                iteration(i, False)

            def out_part(t, i, k):
                n = rows(t)
                for nh in range(2):
                    sl = slice(nh * 512, nh * 512 + 512)
                    if t == TILES - 1:
                        last = passes_sample(ps[OUT_PAIRS[t % 2][nh]][:, :], mid_hi[:, k, SEQ:TP], wo_hi[:, i, sl],
                                             wo_lo[:, i, sl], start=i == 0, stop=i == KT - 1)
                        continue
                    last = passes(ps[OUT_PAIRS[t % 2][nh]][0:n, :], mid_hi[:, k, t * P:t * P + n], mid_lo[:, k, t * P:t * P + n],
                                  wo_hi[:, i, sl], wo_lo[:, i, sl], start=i == 0, stop=i == KT - 1)
                return last

            def transposed(t):
                n = rows(t)
                pe.wait_ge(hw_ready, t + 1)
                if t == TILES - 1:
                    pe.wait_ge(out_taken, TILES - 1)
                elif t >= 2:
                    pe.wait_ge(ht_ready, t - 1)
                for k in range(KT):
                    last = pe.transpose(ps[T3(t)[k // 4]][:, k % 4 * n:k % 4 * n + n],
                                        hw[0:n, t % 2, k * P:(k + 1) * P], ident[0:n, 0:n])
                last.then_inc(ht_done, 1)

            pe.wait_ge(ret_dve, len(BY_DVE) * HEADS)
            for i, k in enumerate(KORDER):
                pe.wait_ge(w_split, H_OUT + 2 * i + 2)
                pe.wait_ge(mix_ready, len(MIX_PARTS) * HEADS - (3 if k >= 4 else 0))
                for t in range(2):
                    last = out_part(t, i, k)
                    if i == KT - 1:
                        last.then_inc(out_done, 1)
            for t in range(2, TILES):
                pe.wait_ge(out_taken, t - 1)
                for i, k in enumerate(KORDER):
                    last = out_part(t, i, k)
                    if i == KT - 1:
                        last.then_inc(out_done, 1)
                    if t == 2 and i == 2:
                        transposed(0)
                    if i == 4:
                        transposed(t - 1)

            def group(g, first):
                for a in range(FT):
                    order = [(0, 0), (0, 1), (0, 2), (1, 0), (1, 1), (1, 2)]
                    if first and a == 0:
                        order = [(0, 0), (0, 1), (1, 0), (1, 1), (0, 2), (1, 2)]
                    for half, j in order:
                        col, w = CGY[j]
                        if j == 0:
                            pe.wait_ge(w_split, ffn_half("up", a, half) + 1 + g * NF)
                        if half == 0:
                            if first and a == 0:
                                pe.wait_ge(ht_ready, [7, 7, 9][j])
                            elif a == 0:
                                pe.wait_ge(down_taken, 9 * g + (0 if j < 2 else 1))
                            elif a == 1:
                                if not first:
                                    pe.wait_ge(relu_done, 12 * g)
                                    pe.wait_ge(down_taken, 9 * g + 1)
                            else:
                                pe.wait_ge(relu_done, 12 * g + 3 * (a - 2) + j + 1)
                        out = ps[a % 2 * 3 + j][:, 0:w]
                        for k in range(4):
                            kk = 4 * half + k
                            last = passes(out, ws_hi[:, half, k, :], ws_lo[:, half, k, :],
                                          mid_hi[:, kk, col:col + w], mid_lo[:, kk, col:col + w],
                                          start=kk == 0, stop=kk == KT - 1)
                        if half == 1:
                            last.then_inc(up_done, 1)
                        elif j == 2:
                            last.then_inc(w_used, 1)
                        if first and a == 0 and (half, j) == (0, 1):
                            transposed(TILES - 1)
                for p, t in enumerate(DOWN_ORDER):
                    n = rows(t)
                    if p == 0:
                        pe.wait_ge(w_split, ffn_half("wd", 3, 1) + 1 + g * NF)
                    pe.wait_ge(f_ready, 12 * g + 9 + 1 + (t * P + n - 1) // BLK)
                    if p == 1:
                        pe.wait_ge(relu_done, 12 * g + 10)
                    elif p == 2:
                        pe.wait_ge(down_taken, 2 + 9 * g)
                    elif p >= 3:
                        pe.wait_ge(down_taken, 2 + 9 * g + p - 2)
                    for nh in range(2):
                        sl = slice(nh * 512, nh * 512 + 512)
                        for a in range(FT):
                            if t == TILES - 1:
                                last = passes_sample(ps[DOWN_PAIRS[p % 3][nh]][:, :], f_hi[:, a, SEQ:TP], wd_hi[:, a, sl],
                                                     wd_lo[:, a, sl], start=a == 0, stop=a == FT - 1)
                                continue
                            last = passes(ps[DOWN_PAIRS[p % 3][nh]][0:n, :], f_hi[:, a, t * P:t * P + n],
                                          f_lo[:, a, t * P:t * P + n], wd_hi[:, a, sl], wd_lo[:, a, sl],
                                          start=a == 0, stop=a == FT - 1)
                        last.then_inc(down_done, 1)

            group(0, True)
            with pe.Fori(1, GROUPS) as g:
                group(g, False)


_INS = ["x_prompt", "x_sample", "state_conv", "state_ret", "meta_tokens", "norm_mix_w", "w_in", "conv_w", "ret_gn_w",
        "w_out", "norm_ffn_w", "w_up", "w_down", "norm_final_w"]
_OUTS = [(1, SEQ, D), (1, SAMPLE, D), (1, 1, 2, DC), (1, 1, HEADS, HD, HD), (1, 1, 2, DC), (1, 1, HEADS, HD, HD)]


def kernel(**inputs):
    import concourse.bacc as bacc
    from concourse.bass_utils import run_bass_kernel_spmd

    nc = bacc.Bacc("TRN2", target_bir_lowering=False, num_devices=1)
    arrays, args = {}, []
    for name, a in [(n, np.ascontiguousarray(inputs[n])) for n in _INS] + list(constants().items()):
        arrays[f"in_{name}"] = a
        args.append(nc.dram_tensor(f"in_{name}", a.shape, mybir.dt.from_np(a.dtype), kind="ExternalInput").ap())
    for i, shape in enumerate(_OUTS):
        args.append(nc.dram_tensor(f"out_{i}", shape, F32, kind="ExternalOutput").ap())
    build(nc, *args)
    r = run_bass_kernel_spmd(nc, [arrays], core_ids=[0])
    return tuple(r.results[0][f"out_{i}"] for i in range(len(_OUTS)))
```
